# Optimizing a Trainium2 kernel written in Bass

```python
import math
import jax, jax.numpy as jnp
from jax import lax
import numpy as np
import math, functools

D_MODEL = 1024
BATCH = 1
SEQ = 512
DEPTH = 2

N_MIXERS = 2
EPS = 1e-6
NEG_INF = -1e30
FORCE_SCORE = 1e9

N_HEADS = 16
HEAD_DIM = 64
N_KV_GROUPS = 4
HEADS_PER_GROUP = N_HEADS // N_KV_GROUPS
ATTN_WIDTH = N_HEADS * HEAD_DIM
KV_WIDTH = N_KV_GROUPS * HEAD_DIM
CMP_BLOCK = 32
CMP_STRIDE = 16
CMP_HIDDEN = 256
SEL_BLOCK = 64
SEL_TOPK = 16
WINDOW = 512
Q_BLOCK = 64
NSA_IN = ATTN_WIDTH + 6 * KV_WIDTH + 3 * N_HEADS + ATTN_WIDTH

SSM_WIDTH = D_MODEL
SSM_GROUP = 16
SSM_GROUPS = SSM_WIDTH // SSM_GROUP
SSM_STATE = 64
SCAN_CHUNK = 128
DT_MIN = 1e-3
DT_MAX = 1e-1


def _rmsnorm(x, g):
    xf = x.astype(jnp.float32)
    y = xf * lax.rsqrt(jnp.mean(xf * xf, axis=-1, keepdims=True) + EPS) * g.astype(jnp.float32)
    return y.astype(x.dtype)

def _masked_softmax(s, mask):
    s = jnp.where(mask, s, NEG_INF)
    m = jnp.max(s, axis=-1, keepdims=True)
    p = jnp.where(mask, jnp.exp(s - m), 0.0)
    return p / jnp.maximum(jnp.sum(p, axis=-1, keepdims=True), 1e-30)

def _alibi_slopes():
    h = jnp.arange(1, N_HEADS + 1, dtype=jnp.float32)
    return jnp.exp2(-8.0 * h / N_HEADS).reshape(N_KV_GROUPS, HEADS_PER_GROUP)

def _compress(k, cmp_idx, pe, w1, w2):
    bsz = k.shape[0]
    n_cmp = cmp_idx.shape[0]
    blk = k[:, cmp_idx] + pe[:, None, :]
    blk = jnp.transpose(blk, (0, 1, 3, 2, 4)).reshape(bsz, n_cmp, N_KV_GROUPS, CMP_BLOCK * HEAD_DIM)
    return jax.nn.silu(blk @ w1) @ w2

def _nsa_mixer(h, w_in, cmp_k_pe, cmp_k_w1, cmp_k_w2, cmp_v_pe, cmp_v_w1, cmp_v_w2, w_out):
    f32 = jnp.float32
    bsz, seq, _ = h.shape
    G, R = N_KV_GROUPS, HEADS_PER_GROUP
    n_cmp = (seq - CMP_BLOCK) // CMP_STRIDE + 1
    n_blocks = seq // SEL_BLOCK
    n_sel = min(SEL_TOPK, n_blocks)

    splits = [ATTN_WIDTH + i * KV_WIDTH for i in range(7)] + [ATTN_WIDTH + 6 * KV_WIDTH + 3 * N_HEADS]
    q, kc, vc, ks, vs, kw, vw, gates, z = jnp.split(h @ w_in, splits, axis=-1)
    q = q.reshape(bsz, seq, G, R, HEAD_DIM) * (HEAD_DIM ** -0.5)
    kc, vc, ks, vs, kw, vw = [a.reshape(bsz, seq, G, HEAD_DIM) for a in (kc, vc, ks, vs, kw, vw)]
    gates = jax.nn.sigmoid(gates.astype(f32)).reshape(bsz, seq, 3, G, R)
    slopes = _alibi_slopes()

    cmp_start = jnp.arange(n_cmp) * CMP_STRIDE
    cmp_idx = cmp_start[:, None] + jnp.arange(CMP_BLOCK)[None, :]
    k_cmp = _compress(kc, cmp_idx, cmp_k_pe, cmp_k_w1, cmp_k_w2)
    v_cmp = _compress(vc, cmp_idx, cmp_v_pe, cmp_v_w1, cmp_v_w2)
    cmp_end = cmp_start + CMP_BLOCK - 1
    cmp_center = cmp_start.astype(f32) + 0.5 * (CMP_BLOCK - 1)

    sel_start = jnp.arange(n_blocks) * SEL_BLOCK
    overlap = ((cmp_start[:, None] <= sel_start[None, :] + SEL_BLOCK - 1)
               & (cmp_end[:, None] >= sel_start[None, :])).astype(f32)

    ks_blk = jnp.transpose(ks.reshape(bsz, n_blocks, SEL_BLOCK, G, HEAD_DIM), (0, 3, 1, 2, 4))
    vs_blk = jnp.transpose(vs.reshape(bsz, n_blocks, SEL_BLOCK, G, HEAD_DIM), (0, 3, 1, 2, 4))
    gather = jax.vmap(jax.vmap(lambda kb, ix: kb[ix]))

    kw_pad = jnp.pad(kw, ((0, 0), (WINDOW, 0), (0, 0), (0, 0)))
    vw_pad = jnp.pad(vw, ((0, 0), (WINDOW, 0), (0, 0), (0, 0)))

    def block(qi):
        q0 = qi * Q_BLOCK
        t = q0 + jnp.arange(Q_BLOCK, dtype=jnp.int32)
        tf = t.astype(f32)
        qb = lax.dynamic_slice_in_dim(q, q0, Q_BLOCK, axis=1)
        gb = lax.dynamic_slice_in_dim(gates, q0, Q_BLOCK, axis=1)

        s_c = jnp.einsum('bqgrd,bngd->bgrqn', qb, k_cmp, preferred_element_type=f32)
        s_c = s_c - slopes[None, :, :, None, None] * (tf[:, None] - cmp_center[None, :])
        p_c = _masked_softmax(s_c, (cmp_end[None, :] <= t[:, None]))
        o_c = jnp.einsum('bgrqn,bngd->bqgrd', p_c, v_cmp)

        imp = jnp.einsum('bgrqn,nj->bgqj', p_c, overlap)
        j = jnp.arange(n_blocks)[None, :]
        jt = (t // SEL_BLOCK)[:, None]
        forced = (j == 0) | (j == jt) | (j == jt - 1)
        imp = jnp.where(forced, FORCE_SCORE, jnp.where(j > jt, -FORCE_SCORE, imp))
        _, sel_idx = lax.top_k(imp, n_sel)

        k_sel = gather(ks_blk, sel_idx)
        v_sel = gather(vs_blk, sel_idx).reshape(bsz, G, Q_BLOCK, n_sel * SEL_BLOCK, HEAD_DIM)
        pos_s = sel_idx[..., None] * SEL_BLOCK + jnp.arange(SEL_BLOCK)
        d_s = t[None, None, :, None, None] - pos_s
        s_s = jnp.einsum('bqgrd,bgqnkd->bgrqnk', qb, k_sel, preferred_element_type=f32)
        s_s = s_s - slopes[None, :, :, None, None, None] * d_s[:, :, None].astype(f32)
        s_s = s_s.reshape(bsz, G, R, Q_BLOCK, n_sel * SEL_BLOCK)
        m_s = (d_s >= 0)[:, :, None].reshape(bsz, G, 1, Q_BLOCK, n_sel * SEL_BLOCK)
        p_s = _masked_softmax(s_s, m_s)
        o_s = jnp.einsum('bgrqm,bgqmd->bqgrd', p_s, v_sel)

        kwb = lax.dynamic_slice_in_dim(kw_pad, q0, Q_BLOCK + WINDOW, axis=1)
        vwb = lax.dynamic_slice_in_dim(vw_pad, q0, Q_BLOCK + WINDOW, axis=1)
        pos_w = q0 - WINDOW + jnp.arange(Q_BLOCK + WINDOW, dtype=jnp.int32)
        d_w = t[:, None] - pos_w[None, :]
        m_w = (pos_w[None, :] >= 0) & (d_w >= 0) & (d_w < WINDOW)
        s_w = jnp.einsum('bqgrd,bkgd->bgrqk', qb, kwb, preferred_element_type=f32)
        s_w = s_w - slopes[None, :, :, None, None] * d_w.astype(f32)
        p_w = _masked_softmax(s_w, m_w)
        o_w = jnp.einsum('bgrqk,bkgd->bqgrd', p_w, vwb)

        return (gb[:, :, 0, :, :, None] * o_c + gb[:, :, 1, :, :, None] * o_s
                + gb[:, :, 2, :, :, None] * o_w)

    o = lax.map(block, jnp.arange(seq // Q_BLOCK, dtype=jnp.int32))
    o = jnp.moveaxis(o, 0, 1).reshape(bsz, seq, ATTN_WIDTH)
    o = (o * jax.nn.silu(z.astype(f32))).astype(h.dtype)
    return o @ w_out

def _complex_affine_combine(left, right):
    ar_i, ai_i, br_i, bi_i = left
    ar_j, ai_j, br_j, bi_j = right
    ar = ar_j * ar_i - ai_j * ai_i
    ai = ar_j * ai_i + ai_j * ar_i
    br = ar_j * br_i - ai_j * bi_i + br_j
    bi = ar_j * bi_i + ai_j * br_i + bi_j
    return ar, ai, br, bi

def _s5_mixer(h, w_in, log_dt, lambda_re, lambda_im, b_re, b_im, c_re, c_im, d_skip, w_glu, w_out):
    f32 = jnp.float32
    bsz, seq, _ = h.shape
    G, C, P = SSM_GROUPS, SSM_GROUP, SSM_STATE
    u, z = jnp.split(h @ w_in, 2, axis=-1)
    u = u.astype(f32).reshape(bsz, seq, G, C)

    dt = jnp.exp(log_dt.astype(f32))[:, None]
    lre = jnp.minimum(lambda_re.astype(f32), -1e-4)
    lim = lambda_im.astype(f32)
    mag = jnp.exp(lre * dt)
    ab_re = mag * jnp.cos(lim * dt)
    ab_im = mag * jnp.sin(lim * dt)
    den = lre * lre + lim * lim
    nr = ab_re - 1.0
    coef_re = (nr * lre + ab_im * lim) / den
    coef_im = (ab_im * lre - nr * lim) / den
    br32, bi32 = b_re.astype(f32), b_im.astype(f32)
    bb_re = coef_re[..., None] * br32 - coef_im[..., None] * bi32
    bb_im = coef_re[..., None] * bi32 + coef_im[..., None] * br32
    cr32, ci32 = c_re.astype(f32), c_im.astype(f32)

    n_chunks = seq // SCAN_CHUNK
    u_chunks = jnp.moveaxis(u.reshape(bsz, n_chunks, SCAN_CHUNK, G, C), 1, 0)
    a_re = jnp.broadcast_to(ab_re, (bsz, SCAN_CHUNK, G, P))
    a_im = jnp.broadcast_to(ab_im, (bsz, SCAN_CHUNK, G, P))

    def chunk_step(carry, u_c):
        x_re, x_im = carry
        bu_re = jnp.einsum('gpc,bkgc->bkgp', bb_re, u_c)
        bu_im = jnp.einsum('gpc,bkgc->bkgp', bb_im, u_c)
        ar, ai, sr, si = lax.associative_scan(_complex_affine_combine, (a_re, a_im, bu_re, bu_im), axis=1)
        xr = sr + ar * x_re[:, None] - ai * x_im[:, None]
        xi = si + ar * x_im[:, None] + ai * x_re[:, None]
        y = jnp.einsum('gcp,bkgp->bkgc', cr32, xr) - jnp.einsum('gcp,bkgp->bkgc', ci32, xi)
        return (xr[:, -1], xi[:, -1]), y

    x0 = jnp.zeros((bsz, G, P), f32)
    _, y = lax.scan(chunk_step, (x0, x0), u_chunks)
    y = jnp.moveaxis(y, 0, 1).reshape(bsz, seq, G, C) + d_skip.astype(f32) * u
    y = jax.nn.gelu(y.reshape(bsz, seq, SSM_WIDTH)).astype(h.dtype)
    ga, gb = jnp.split(y @ w_glu, 2, axis=-1)
    y = ga * jax.nn.sigmoid(gb)
    y = y * jax.nn.silu(z)
    return y @ w_out

def _normal(key, shape, scale):
    return jax.random.normal(key, shape, jnp.float32) * scale

def _nsa_params(key, p):
    ks = jax.random.split(key, 9)
    return {
        p + 'norm': 1.0 + _normal(ks[0], (D_MODEL,), 0.02),
        p + 'w_in': _normal(ks[1], (D_MODEL, NSA_IN), D_MODEL ** -0.5),
        p + 'cmp_k_pe': _normal(ks[2], (CMP_BLOCK, HEAD_DIM), 0.02),
        p + 'cmp_k_w1': _normal(ks[3], (CMP_BLOCK * HEAD_DIM, CMP_HIDDEN), (CMP_BLOCK * HEAD_DIM) ** -0.5),
        p + 'cmp_k_w2': _normal(ks[4], (CMP_HIDDEN, HEAD_DIM), CMP_HIDDEN ** -0.5),
        p + 'cmp_v_pe': _normal(ks[5], (CMP_BLOCK, HEAD_DIM), 0.02),
        p + 'cmp_v_w1': _normal(ks[6], (CMP_BLOCK * HEAD_DIM, CMP_HIDDEN), (CMP_BLOCK * HEAD_DIM) ** -0.5),
        p + 'cmp_v_w2': _normal(ks[7], (CMP_HIDDEN, HEAD_DIM), CMP_HIDDEN ** -0.5),
        p + 'w_out': _normal(ks[8], (ATTN_WIDTH, D_MODEL), ATTN_WIDTH ** -0.5),
    }

def _s5_params(key, p):
    ks = jax.random.split(key, 12)
    n = jnp.arange(SSM_STATE, dtype=jnp.float32)[None, :]
    return {
        p + 'norm': 1.0 + _normal(ks[0], (D_MODEL,), 0.02),
        p + 'w_in': _normal(ks[1], (D_MODEL, 2 * SSM_WIDTH), D_MODEL ** -0.5),
        p + 'log_dt': jax.random.uniform(ks[2], (SSM_GROUPS,), jnp.float32, math.log(DT_MIN), math.log(DT_MAX)),
        p + 'lambda_re': -0.5 + _normal(ks[3], (SSM_GROUPS, SSM_STATE), 0.01),
        p + 'lambda_im': math.pi * n + _normal(ks[4], (SSM_GROUPS, SSM_STATE), 0.01),
        p + 'b_re': _normal(ks[5], (SSM_GROUPS, SSM_STATE, SSM_GROUP), (2 * SSM_GROUP) ** -0.5),
        p + 'b_im': _normal(ks[6], (SSM_GROUPS, SSM_STATE, SSM_GROUP), (2 * SSM_GROUP) ** -0.5),
        p + 'c_re': _normal(ks[7], (SSM_GROUPS, SSM_GROUP, SSM_STATE), SSM_STATE ** -0.5),
        p + 'c_im': _normal(ks[8], (SSM_GROUPS, SSM_GROUP, SSM_STATE), SSM_STATE ** -0.5),
        p + 'd': _normal(ks[9], (SSM_GROUPS, SSM_GROUP), 1.0),
        p + 'w_glu': _normal(ks[10], (SSM_WIDTH, 2 * SSM_WIDTH), SSM_WIDTH ** -0.5),
        p + 'w_out': _normal(ks[11], (SSM_WIDTH, D_MODEL), SSM_WIDTH ** -0.5),
    }

def first_inputs(seed: int = 0) -> dict:
    key = jax.random.key(seed)
    kx, k0, k1, k2, k3, kf = jax.random.split(key, 6)
    inputs = {'x': jax.random.normal(kx, (BATCH, SEQ, D_MODEL), jnp.float32)}
    inputs.update(_nsa_params(k0, 'l0_'))
    inputs.update(_s5_params(k1, 'l1_'))
    inputs.update(_nsa_params(k2, 'l2_'))
    inputs.update(_s5_params(k3, 'l3_'))
    inputs['final_norm'] = 1.0 + _normal(kf, (D_MODEL,), 0.02)
    return inputs

def first_block(x,
              l0_norm, l0_w_in, l0_cmp_k_pe, l0_cmp_k_w1, l0_cmp_k_w2, l0_cmp_v_pe, l0_cmp_v_w1, l0_cmp_v_w2, l0_w_out,
              l1_norm, l1_w_in, l1_log_dt, l1_lambda_re, l1_lambda_im, l1_b_re, l1_b_im, l1_c_re, l1_c_im, l1_d, l1_w_glu, l1_w_out,
              l2_norm, l2_w_in, l2_cmp_k_pe, l2_cmp_k_w1, l2_cmp_k_w2, l2_cmp_v_pe, l2_cmp_v_w1, l2_cmp_v_w2, l2_w_out,
              l3_norm, l3_w_in, l3_log_dt, l3_lambda_re, l3_lambda_im, l3_b_re, l3_b_im, l3_c_re, l3_c_im, l3_d, l3_w_glu, l3_w_out,
              final_norm):
    nsa_layers = [
        (l0_norm, l0_w_in, l0_cmp_k_pe, l0_cmp_k_w1, l0_cmp_k_w2, l0_cmp_v_pe, l0_cmp_v_w1, l0_cmp_v_w2, l0_w_out),
        (l2_norm, l2_w_in, l2_cmp_k_pe, l2_cmp_k_w1, l2_cmp_k_w2, l2_cmp_v_pe, l2_cmp_v_w1, l2_cmp_v_w2, l2_w_out),
    ]
    s5_layers = [
        (l1_norm, l1_w_in, l1_log_dt, l1_lambda_re, l1_lambda_im, l1_b_re, l1_b_im, l1_c_re, l1_c_im, l1_d, l1_w_glu, l1_w_out),
        (l3_norm, l3_w_in, l3_log_dt, l3_lambda_re, l3_lambda_im, l3_b_re, l3_b_im, l3_c_re, l3_c_im, l3_d, l3_w_glu, l3_w_out),
    ]
    h = x
    for i in range(DEPTH):
        if i % N_MIXERS == 0:
            params = nsa_layers[i // N_MIXERS]
            y = _nsa_mixer(_rmsnorm(h, params[0]), *params[1:])
        else:
            params = s5_layers[i // N_MIXERS]
            y = _s5_mixer(_rmsnorm(h, params[0]), *params[1:])
        h = h + y.astype(h.dtype)
    return _rmsnorm(h, final_norm)


SB_HEADS = 8
SB_HEAD_DIM = 64
SB_WIDTH = SB_HEADS * SB_HEAD_DIM
RET_HEADS = 4
RET_HEAD_DIM = 128
RET_WIDTH = RET_HEADS * RET_HEAD_DIM
EVEN_IN = 3 * SB_WIDTH + 4 * RET_WIDTH
GLA_HEADS = 4
GLA_DK = 128
GLA_DV = 256
GLA_K_WIDTH = GLA_HEADS * GLA_DK
GLA_V_WIDTH = GLA_HEADS * GLA_DV
GLA_GATE_RANK = 16
GLA_GATE_TAU = 16.0
ODD_IN = 2 * GLA_K_WIDTH + 2 * GLA_V_WIDTH + GLA_GATE_RANK
D_FF = 2816
CONV_WIDTH = 3
Q_BLOCK_2 = 128
RET_CHUNK = 128
GLA_CHUNK = 64
ROPE_BASE = 10000.0
N_EVEN = (DEPTH + 1) // 2
N_ODD = DEPTH // 2


def rms_norm(x, g):
    xf = x.astype(jnp.float32)
    y = xf * lax.rsqrt(jnp.mean(xf * xf, axis=-1, keepdims=True) + EPS)
    return (y * g.astype(jnp.float32)).astype(x.dtype)

def to_heads(t, n):
    b, s, w = t.shape
    return t.reshape(b, s, n, w // n).transpose(0, 2, 1, 3)

def from_heads(t):
    b, h, s, d = t.shape
    return t.transpose(0, 2, 1, 3).reshape(b, s, h * d)

def rope(x, pos):
    d = x.shape[-1]
    half = d // 2
    inv = ROPE_BASE ** (-jnp.arange(half, dtype=jnp.float32) / half)
    ang = pos.astype(jnp.float32)[:, None] * inv[None, :]
    cos, sin = jnp.cos(ang), jnp.sin(ang)
    xf = x.astype(jnp.float32)
    x1, x2 = xf[..., :half], xf[..., half:]
    return jnp.concatenate([x1 * cos - x2 * sin, x1 * sin + x2 * cos], axis=-1).astype(x.dtype)

def stick_breaking_attention(q, k, v):
    b, h, s, d = q.shape
    nb = s // Q_BLOCK_2
    scale = d ** -0.5
    qb = q.reshape(b, h, nb, Q_BLOCK_2, d).transpose(2, 0, 1, 3, 4)
    kf = k.astype(jnp.float32)
    vf = v.astype(jnp.float32)
    key_pos = jnp.arange(s)

    def block(args):
        qi, i = args
        q_pos = i * Q_BLOCK_2 + jnp.arange(Q_BLOCK_2)
        z = jnp.einsum('bhqd,bhkd->bhqk', qi.astype(jnp.float32), kf) * scale
        mask = key_pos[None, :] < q_pos[:, None]
        log_beta = jax.nn.log_sigmoid(z)
        log_1m_beta = jnp.where(mask, -jax.nn.softplus(z), 0.0)
        suffix = lax.cumsum(log_1m_beta, axis=3, reverse=True) - log_1m_beta
        w = jnp.where(mask, jnp.exp(log_beta + suffix), 0.0)
        return jnp.einsum('bhqk,bhkd->bhqd', w, vf)

    out = lax.map(block, (qb, jnp.arange(nb)))
    return out.transpose(1, 2, 0, 3, 4).reshape(b, h, s, d).astype(v.dtype)

def retention_chunkwise(q, k, v, log_gamma):
    b, h, s, d = q.shape
    c = RET_CHUNK
    nc = s // c
    qc = q.astype(jnp.float32).reshape(b, h, nc, c, d)
    kc = (k.astype(jnp.float32) * d ** -0.5).reshape(b, h, nc, c, d)
    vc = v.astype(jnp.float32).reshape(b, h, nc, c, d)
    pos = jnp.arange(c, dtype=jnp.float32)
    lg = log_gamma[:, None]
    diff = pos[:, None] - pos[None, :]
    decay_intra = jnp.where(diff >= 0, jnp.exp(lg[:, :, None] * jnp.maximum(diff, 0.0)), 0.0)
    scores = jnp.einsum('bhnid,bhnjd->bhnij', qc, kc) * decay_intra[None, :, None]
    inner = jnp.einsum('bhnij,bhnje->bhnie', scores, vc)
    zeta = jnp.exp(lg * (c - 1 - pos))
    contrib = jnp.einsum('bhnjd,hj,bhnje->bhnde', kc, zeta, vc)
    g_chunk = jnp.exp(lg * c)[None, :, :, None]

    def step(state, cn):
        return g_chunk * state + cn, state

    _, r_prev = lax.scan(step, jnp.zeros((b, h, d, d), jnp.float32), contrib.transpose(2, 0, 1, 3, 4))
    r_prev = r_prev.transpose(1, 2, 0, 3, 4)
    xi = jnp.exp(lg * (pos + 1.0))
    cross = jnp.einsum('bhnid,bhnde->bhnie', qc, r_prev) * xi[None, :, None, :, None]
    return (inner + cross).reshape(b, h, s, d).astype(v.dtype)

def gla_chunked(q, k, v, log_alpha):
    b, h, s, dk = q.shape
    dv = v.shape[-1]
    c = GLA_CHUNK
    nc = s // c
    qc = (q.astype(jnp.float32) * dk ** -0.5).reshape(b, h, nc, c, dk)
    kc = k.astype(jnp.float32).reshape(b, h, nc, c, dk)
    vc = v.astype(jnp.float32).reshape(b, h, nc, c, dv)
    cum = lax.cumsum(log_alpha.astype(jnp.float32).reshape(b, h, nc, c, dk), axis=3)
    cum_last = cum[:, :, :, -1:, :]
    q_t = qc * jnp.exp(cum)
    k_t = kc * jnp.exp(-cum)
    causal = jnp.tril(jnp.ones((c, c), dtype=bool))
    a = jnp.where(causal, jnp.einsum('bhnid,bhnjd->bhnij', q_t, k_t), 0.0)
    intra = jnp.einsum('bhnij,bhnje->bhnie', a, vc)
    contrib = jnp.einsum('bhnjd,bhnje->bhnde', kc * jnp.exp(cum_last - cum), vc)
    chunk_decay = jnp.exp(cum_last[:, :, :, 0, :])

    def step(state, inp):
        dec, cn = inp
        return dec[..., None] * state + cn, state

    _, s_prev = lax.scan(step, jnp.zeros((b, h, dk, dv), jnp.float32),
                         (chunk_decay.transpose(2, 0, 1, 3), contrib.transpose(2, 0, 1, 3, 4)))
    s_prev = s_prev.transpose(1, 2, 0, 3, 4)
    inter = jnp.einsum('bhnid,bhnde->bhnie', q_t, s_prev)
    return (intra + inter).reshape(b, h, s, dv).astype(v.dtype)

def even_mixer(hn, w_in, q_gain, k_gain, ret_gain, w_out):
    s = hn.shape[1]
    p = hn @ w_in
    cuts = [SB_WIDTH, 2 * SB_WIDTH, 3 * SB_WIDTH,
            3 * SB_WIDTH + RET_WIDTH, 3 * SB_WIDTH + 2 * RET_WIDTH, 3 * SB_WIDTH + 3 * RET_WIDTH]
    sb_q, sb_k, sb_v, r_q, r_k, r_v, r_g = jnp.split(p, cuts, axis=-1)
    qa = rms_norm(to_heads(sb_q, SB_HEADS), q_gain)
    ka = rms_norm(to_heads(sb_k, SB_HEADS), k_gain)
    out_a = from_heads(stick_breaking_attention(qa, ka, to_heads(sb_v, SB_HEADS)))
    pos = jnp.arange(s)
    qb = rope(to_heads(r_q, RET_HEADS), pos)
    kb = rope(to_heads(r_k, RET_HEADS), pos)
    log_gamma = jnp.log(1.0 - jnp.exp2(-5.0 - jnp.arange(RET_HEADS, dtype=jnp.float32)))
    ret = retention_chunkwise(qb, kb, to_heads(r_v, RET_HEADS), log_gamma)
    out_b = from_heads(rms_norm(ret, ret_gain)) * jax.nn.silu(r_g)
    return jnp.concatenate([out_a, out_b], axis=-1) @ w_out

def odd_mixer(hn, w_in, w_alpha, b_alpha, out_gain, w_out):
    p = hn @ w_in
    cuts = [GLA_K_WIDTH, 2 * GLA_K_WIDTH, 2 * GLA_K_WIDTH + GLA_V_WIDTH, 2 * GLA_K_WIDTH + 2 * GLA_V_WIDTH]
    g_q, g_k, g_v, g_r, g_a = jnp.split(p, cuts, axis=-1)
    log_alpha = jax.nn.log_sigmoid((g_a @ w_alpha + b_alpha).astype(jnp.float32)) / GLA_GATE_TAU
    o = gla_chunked(to_heads(g_q, GLA_HEADS), to_heads(g_k, GLA_HEADS),
                    to_heads(g_v, GLA_HEADS), to_heads(log_alpha, GLA_HEADS))
    return (from_heads(rms_norm(o, out_gain)) * jax.nn.silu(g_r)) @ w_out

def conv_ffn(hn, w_up, conv_w, conv_b, w_down):
    s = hn.shape[1]
    u, v = jnp.split(hn @ w_up, 2, axis=-1)
    up = jnp.pad(u, ((0, 0), (CONV_WIDTH - 1, 0), (0, 0)))
    uc = conv_b + conv_w[0] * up[:, 0:s]
    for j in range(1, CONV_WIDTH):
        uc = uc + conv_w[j] * up[:, j:j + s]
    return (jax.nn.silu(uc) * v) @ w_down

def second_inputs(seed: int = 0) -> dict:
    key = jax.random.key(seed)
    ks = jax.random.split(key, 20)
    f32 = jnp.float32

    def nrm(k, shape, scale):
        return jax.random.normal(k, shape, f32) * scale

    return {
        'x': nrm(ks[0], (BATCH, SEQ, D_MODEL), 1.0),
        'mix_norm_g': 1.0 + nrm(ks[1], (DEPTH, D_MODEL), 0.02),
        'even_w_in': nrm(ks[2], (N_EVEN, D_MODEL, EVEN_IN), D_MODEL ** -0.5),
        'sb_q_gain': 1.0 + nrm(ks[3], (N_EVEN, SB_HEAD_DIM), 0.02),
        'sb_k_gain': 1.0 + nrm(ks[4], (N_EVEN, SB_HEAD_DIM), 0.02),
        'ret_out_gain': 1.0 + nrm(ks[5], (N_EVEN, RET_HEAD_DIM), 0.02),
        'even_w_out': nrm(ks[6], (N_EVEN, SB_WIDTH + RET_WIDTH, D_MODEL), (SB_WIDTH + RET_WIDTH) ** -0.5),
        'odd_w_in': nrm(ks[7], (N_ODD, D_MODEL, ODD_IN), D_MODEL ** -0.5),
        'gla_w_alpha': nrm(ks[8], (N_ODD, GLA_GATE_RANK, GLA_K_WIDTH), GLA_GATE_RANK ** -0.5),
        'gla_b_alpha': nrm(ks[9], (N_ODD, GLA_K_WIDTH), 0.1),
        'gla_out_gain': 1.0 + nrm(ks[10], (N_ODD, GLA_DV), 0.02),
        'odd_w_out': nrm(ks[11], (N_ODD, GLA_V_WIDTH, D_MODEL), GLA_V_WIDTH ** -0.5),
        'ffn_norm_g': 1.0 + nrm(ks[12], (DEPTH, D_MODEL), 0.02),
        'ffn_w_up': nrm(ks[13], (DEPTH, D_MODEL, 2 * D_FF), D_MODEL ** -0.5),
        'ffn_conv_w': nrm(ks[14], (DEPTH, CONV_WIDTH, D_FF), CONV_WIDTH ** -0.5),
        'ffn_conv_b': nrm(ks[15], (DEPTH, D_FF), 0.01),
        'ffn_w_down': nrm(ks[16], (DEPTH, D_FF, D_MODEL), D_FF ** -0.5),
    }

def second_block(x, mix_norm_g, even_w_in, sb_q_gain, sb_k_gain, ret_out_gain, even_w_out,
              odd_w_in, gla_w_alpha, gla_b_alpha, gla_out_gain, odd_w_out,
              ffn_norm_g, ffn_w_up, ffn_conv_w, ffn_conv_b, ffn_w_down):
    h = x
    for layer in range(DEPTH):
        hn = rms_norm(h, mix_norm_g[layer])
        if layer % 2 == 0:
            e = layer // 2
            mix = even_mixer(hn, even_w_in[e], sb_q_gain[e], sb_k_gain[e], ret_out_gain[e], even_w_out[e])
        else:
            o = layer // 2
            mix = odd_mixer(hn, odd_w_in[o], gla_w_alpha[o], gla_b_alpha[o], gla_out_gain[o], odd_w_out[o])
        h = h + mix.astype(h.dtype)
        hn = rms_norm(h, ffn_norm_g[layer])
        h = h + conv_ffn(hn, ffn_w_up[layer], ffn_conv_w[layer], ffn_conv_b[layer], ffn_w_down[layer]).astype(h.dtype)
    return h


def setup_inputs(seed=0):
    out = dict(first_inputs(seed))
    for name, value in second_inputs(seed + 1).items():
        if name != "x":
            out[name + "_2"] = value
    return out


def reference(
    x, l0_norm, l0_w_in, l0_cmp_k_pe, l0_cmp_k_w1, l0_cmp_k_w2, l0_cmp_v_pe, l0_cmp_v_w1,
    l0_cmp_v_w2, l0_w_out, l1_norm, l1_w_in, l1_log_dt, l1_lambda_re, l1_lambda_im, l1_b_re,
    l1_b_im, l1_c_re, l1_c_im, l1_d, l1_w_glu, l1_w_out, l2_norm, l2_w_in, l2_cmp_k_pe,
    l2_cmp_k_w1, l2_cmp_k_w2, l2_cmp_v_pe, l2_cmp_v_w1, l2_cmp_v_w2, l2_w_out, l3_norm, l3_w_in,
    l3_log_dt, l3_lambda_re, l3_lambda_im, l3_b_re, l3_b_im, l3_c_re, l3_c_im, l3_d, l3_w_glu,
    l3_w_out, final_norm, mix_norm_g_2, even_w_in_2, sb_q_gain_2, sb_k_gain_2, ret_out_gain_2,
    even_w_out_2, odd_w_in_2, gla_w_alpha_2, gla_b_alpha_2, gla_out_gain_2, odd_w_out_2,
    ffn_norm_g_2, ffn_w_up_2, ffn_conv_w_2, ffn_conv_b_2, ffn_w_down_2,
):
    x = first_block(
        x, l0_norm, l0_w_in, l0_cmp_k_pe, l0_cmp_k_w1, l0_cmp_k_w2, l0_cmp_v_pe, l0_cmp_v_w1,
        l0_cmp_v_w2, l0_w_out, l1_norm, l1_w_in, l1_log_dt, l1_lambda_re, l1_lambda_im, l1_b_re,
        l1_b_im, l1_c_re, l1_c_im, l1_d, l1_w_glu, l1_w_out, l2_norm, l2_w_in, l2_cmp_k_pe,
        l2_cmp_k_w1, l2_cmp_k_w2, l2_cmp_v_pe, l2_cmp_v_w1, l2_cmp_v_w2, l2_w_out, l3_norm,
        l3_w_in, l3_log_dt, l3_lambda_re, l3_lambda_im, l3_b_re, l3_b_im, l3_c_re, l3_c_im,
        l3_d, l3_w_glu, l3_w_out, final_norm,
    )
    return second_block(
        x, mix_norm_g_2, even_w_in_2, sb_q_gain_2, sb_k_gain_2, ret_out_gain_2, even_w_out_2,
        odd_w_in_2, gla_w_alpha_2, gla_b_alpha_2, gla_out_gain_2, odd_w_out_2, ffn_norm_g_2,
        ffn_w_up_2, ffn_conv_w_2, ffn_conv_b_2, ffn_w_down_2,
    )


_drawn_inputs = setup_inputs


def setup_inputs(seed=0):
    import zlib

    import numpy as np

    out = dict(_drawn_inputs(seed))
    spreads = {}
    factors = {'l0_norm': 4.307,
     'l0_cmp_k_pe': 8.0,
     'l0_cmp_v_pe': 8.0,
     'l1_norm': 5.506,
     'l1_lambda_re': 34.076,
     'l1_b_re': 2.893,
     'l1_b_im': 2.874,
     'l1_c_re': 2.891,
     'l1_c_im': 2.887,
     'sb_q_gain_2': 8.0,
     'sb_k_gain_2': 8.0,
     'ret_out_gain_2': 4.869,
     'gla_b_alpha_2': 3.188,
     'gla_out_gain_2': 20.199,
     'ffn_conv_b_2': 7.995,
     'ffn_norm_g_2': 3.989}
    for name, (base, spread) in spreads.items():
        noise = np.random.default_rng([zlib.crc32(name.encode()), seed]).standard_normal(out[name].shape)
        drawn = base * np.exp(spread * noise) if base else spread * noise
        out[name] = __import__('jax').numpy.asarray(drawn.astype(out[name].dtype))
    for name, factor in factors.items():
        out[name] = (out[name] * factor).astype(out[name].dtype)
    return out
```

```python
from contextlib import ExitStack

import numpy as np
import concourse.bass as bass
from concourse import mybir

F32 = mybir.dt.float32
F32R = mybir.dt.float32r
ALU = mybir.AluOpType
ACT = mybir.ActivationFunctionType
AX = mybir.AxisListType
ds = bass.ds

P = 128
S = 512
D = 1024
KC = D // P
EPS = 1e-6
DFF = 2816
FT = DFF // P
RING = 4
SLAB = KC * P

N_NSA, N_S5, N_FINAL, N_MIX0, N_FFN0, N_MIX1, N_FFN1 = range(7)
NORMS = 7
LOG_EXP = "natural_log_exp_and_others"

STAGES = [("nsa_kv", 8, 1), ("cmp", 8, 2), ("nsa_rest", 20, 1), ("nsa_out", 8, 1),
          ("s5_in", 16, 1), ("s5_glu", 16, 1), ("s5_out", 8, 1),
          ("even_in", 28, 1), ("even_out", 8, 1), ("up0", 2 * FT, 1), ("down0", 24, 3),
          ("odd_in", 24, 1), ("odd_out", 8, 1), ("up1", 2 * FT, 1), ("down1", 24, 3)]


def plan(names):
    t0, o0, n, t, o = {}, {}, {}, 0, 0
    for name, tiles, per_output in STAGES:
        if name not in names:
            continue
        t0[name], o0[name], n[name] = t, o, tiles
        t, o = t + tiles, o + tiles // per_output
    return t0, o0, n, t


def build(nc, A, out, names=tuple(s[0] for s in STAGES)):
    T0, O0, NT, TILES = plan(names)
    norms = [n for n, stage in enumerate(("nsa_kv", "s5_in", "s5_in", "even_in", "up0", "odd_in", "up1"))
             if stage in names]
    ORDER = {key: n for n, key in enumerate(norms)}

    with ExitStack() as ctx:
        def sb(name, shape, dt=F32):
            return ctx.enter_context(nc.sbuf_tensor(name, shape, dt))

        def sem(name):
            return ctx.enter_context(nc.semaphore(name))

        bank = [ctx.enter_context(nc.psum_tensor(f"bank{b}", [P, S], F32)) for b in range(8)]
        acc = bank[0:2]
        ssum = bank[7]

        h = sb("h", [P, KC, S])
        xh = sb("xh", [P, KC, S], F32R)
        xl = sb("xl", [P, KC, S], F32R)
        raw = sb("raw", [P, RING, SLAB])
        whi = sb("whi", [P, 2, SLAB], F32R)
        wlo = sb("wlo", [P, 2, SLAB], F32R)
        tables = sb("tables", [P, A["tables"].shape[1]])
        gains = sb("gains", [P, NORMS, KC])
        sq = sb("sq", [P, 2, S])
        xf = sb("xf", [P, 2, S])
        lnv = sb("lnv", [P, S])
        rstd = sb("rstd", [P, S])
        seedt = sb("seedt", [P, 64])
        xzero = sb("xzero", [P, S])
        ones = tables[:, 0:P]
        ident = tables[:, P:2 * P]
        epsc = tables[:, 2 * P:2 * P + 1]
        base = (nc.sbuf_base + 63) // 64 * 64
        used = [base]

        def at(name, shape, dt=F32, offset=None):
            size = int(np.prod(shape[1:])) * 4
            offset = used[0] if offset is None else offset
            used[0] = offset + (size + 63) // 64 * 64
            assert used[0] <= nc.sbuf_usable_end, (name, used[0])
            return nc.alloc_sbuf_tensor_at(name, shape, dt, offset=offset)

        w_landed = [sem(f"w_landed{s}") for s in range(RING)]
        w_hi = sem("w_hi")
        w_lo = sem("w_lo")
        tile_done = sem("tile_done")
        acc_free = [sem("acc_free0"), sem("acc_free1")]
        loaded = sem("loaded")
        x_landed = sem("x_landed")
        sq_ready = sem("sq_ready")
        ss_done = sem("ss_done")
        ln_ready = sem("ln_ready")
        rstd_ready = sem("rstd_ready")
        norm_f = sem("norm_f")
        norm_hi = sem("norm_hi")
        norm_lo = sem("norm_lo")
        out_written = sem("out_written")
        zeroed = sem("zeroed")

        def sp_stream(sp):
            for t in range(RING):
                sp.dma_start(raw[:, t, :], A["weights"][t]).then_inc(w_landed[t], 16)
            with sp.Fori(1, TILES // RING) as i:
                for s in range(RING):
                    sp.wait_ge(w_lo, i * RING + (s - RING + 1))
                    sp.dma_start(raw[:, s, :], A["weights"][ds(i * RING + s, 1)]
                                 .rearrange("a p n -> (a p) n")).then_inc(w_landed[s], 16)

        def pool_stream(pool, first, last):
            with pool.Fori(0, (last - first) // RING) as i:
                for s in range(RING):
                    pool.wait_ge(w_hi, i * RING + (first + s + 1))
                    nc.gpsimd.tensor_tensor(wlo[:, s % 2, :], raw[:, s, :], whi[:, s % 2, :].bitcast(F32),
                                            ALU.subtract).then_inc(w_lo, 1)

        def split_tile(dve, t_of_4, group, first=False):
            dve.wait_ge(w_landed[t_of_4], (group + 1) * 16)
            nc.vector.tensor_copy(whi[:, t_of_4 % 2, :], raw[:, t_of_4, :]).then_inc(w_hi, 1)

        def product(pe, par, to, rhs_hi, rhs_lo, chunks, first, last):
            for k in range(chunks):
                w_h, w_l = whi[:, par, k * P:(k + 1) * P], wlo[:, par, k * P:(k + 1) * P]
                pe_h, pe_l = rhs_hi(k), rhs_lo(k)
                nc.tensor.matmul(to, w_h, pe_h, start=first and k == 0, stop=False)
                nc.tensor.matmul(to, w_h, pe_l, start=False, stop=False)
                last_mm = nc.tensor.matmul(to, w_l, pe_h, start=False, stop=last and k == chunks - 1)
            return last_mm

        def products_feature_major(pe, stage, skip, n, body=4):
            t0, o0 = T0[stage] + skip, O0[stage] + skip
            with pe.Fori(0, n // body) as i:
                for j in range(body):
                    pe.wait_ge(w_lo, i * body + (t0 + j + 1))
                    pe.wait_ge(acc_free[j % 2], i * (body // 2) + ((o0 + j) // 2 + 1))
                    product(pe, j % 2, acc[j % 2][:], lambda k: xh[:, k, :], lambda k: xl[:, k, :],
                            KC, True, True).then_inc(tile_done, 1)

        def splits_only(dve, stage, skip, n, body=4):
            t0 = T0[stage] + skip
            with dve.Fori(0, n // body) as i:
                for j in range(body):
                    dve.wait_ge(tile_done, i * body + (t0 + j + 1))
                    split_tile(dve, (j + 2) % 4, i * (body // 4) + ((t0 + j + 2) // 4))

        SQ, SS = 9, 10
        splitting = [n for n in range(len(norms)) if norms[n] != N_FINAL]
        SPLIT = {n: k for k, n in enumerate(splitting)}

        def chunk(x, m):
            return x[:, ds(m, 1), :].rearrange("p a s -> p (a s)")

        def act_zero_square(act, n):
            if n:
                act.wait_ge(ss_done, SS * n)
            nc.scalar.activation(sq[:, 1, :], xzero[:], ACT.Copy).then_inc(sq_ready, 1)

        def act_square(act, n, m, j):
            act.wait_ge(ss_done, m + (SS * n + 1))
            nc.scalar.activation(sq[:, j % 2, :], chunk(h, m), ACT.Square).then_inc(sq_ready, 1)

        def pe_squares_start(pe, n):
            pe.wait_ge(sq_ready, SQ * n + 1)
            if n:
                pe.wait_ge(ln_ready, n)
            nc.tensor.matmul(ssum[:], ones, sq[:, 1, :], start=True, stop=False).then_inc(ss_done, 1)

        def pe_squares(pe, squares, par, last=False):
            pe.wait_ge(sq_ready, squares)
            nc.tensor.matmul(ssum[:], ones, sq[:, par, :], start=False, stop=last).then_inc(ss_done, 1)

        def pe_all_squares(pe, n):
            pe_squares_start(pe, n)
            with pe.Fori(0, 4) as i:
                for j in range(2):
                    pe_squares(pe, i * 2 + (SQ * n + j + 1), (j + 1) % 2)
            pe_squares(pe, SQ * n + 9, 1, last=True)

        def act_all_squares(act, n, ready, count):
            act_zero_square(act, n)
            with act.Fori(0, 4) as i:
                for j in range(2):
                    if count is not None:
                        act.wait_ge(ready, count(i * 2 + j))
                    act_square(act, n, i * 2 + j, j)

        def act_rstd(act, n):
            act.wait_ge(ss_done, SS * (n + 1))
            if n:
                act.wait_ge(norm_f, 8 * n)
            act.preload_act_table_set(LOG_EXP)
            nc.scalar.activation(lnv[:], ssum[:], ACT.Ln, bias=epsc, scale=1.0 / D).then_inc(ln_ready, 1)
            act.wait_ge(ln_ready, n + 1)
            nc.scalar.activation(rstd[:], lnv[:], ACT.Exp, scale=-0.5).then_inc(rstd_ready, 1)

        def act_norm_split(act, n, to=None):
            with act.Fori(0, KC // 2) as i:
                for j in range(2):
                    act.wait_ge(norm_f, i * 2 + (8 * n + j + 1))
                    nc.scalar.activation(chunk(xh, i * 2 + j), xf[:, j, :], ACT.Copy).then_inc(norm_hi, 1)

        def dve_norm(dve, n, view=lambda x: x, reader=None):
            dve.wait_ge(rstd_ready, n + 1)
            with dve.Fori(0, KC // 2) as i:
                for j in range(2):
                    dve.wait_ge(norm_lo, i * 2 + (8 * SPLIT[n] + j + 1))
                    if reader is not None:
                        dve.wait_ge(reader, i * 2 + (j + 1))
                    nc.vector.scalar_tensor_tensor(view(xf[:, j, :]), chunk(h, i * 2 + j), gains[:, norms[n], ds(i * 2 + j, 1)],
                                                   rstd[:], ALU.mult, ALU.mult).then_inc(norm_f, 1)
                for j in range(2):
                    dve.wait_ge(norm_hi, i * 2 + (8 * SPLIT[n] + j + 1))
                    nc.vector.tensor_tensor(chunk(xl, i * 2 + j), xf[:, j, :], chunk(xh, i * 2 + j).bitcast(F32),
                                            ALU.subtract).then_inc(norm_lo, 1)

        def pe_normed(pe, n):
            pe.wait_ge(norm_lo, 8 * (SPLIT[n] + 1) + 2)

        def freed(o, i=0, per=0):
            return i * per + (o // 2 + 2)

        def pe_residual(pe, stage, n, per=1, rhs=None, chunks=(KC,)):
            rhs = rhs or [(lambda k: xh[:, k, :], lambda k: xl[:, k, :])]
            t0, o0 = T0[stage], O0[stage]
            if n is not None:
                pe_squares_start(pe, n)
            with pe.Fori(0, 2) as i:
                for j in range(4):
                    for q in range(per):
                        pe.wait_ge(w_lo, i * (4 * per) + (t0 + j * per + q + 1))
                        if q == 0:
                            pe.wait_ge(acc_free[j % 2], i * 2 + ((o0 + j) // 2 + 1))
                        product(pe, (j * per + q) % 2, acc[j % 2][:], *rhs[q], chunks[q],
                                q == 0, q == per - 1).then_inc(tile_done, 1)
                    if n is not None:
                        pe_squares(pe, i * 4 + (SQ * n + j + 1), (j + 1) % 2)
            if n is not None:
                pe_squares(pe, SQ * n + 9, 1, last=True)

        def dve_residual(dve, stage, per=1, view=lambda x: x):
            t0 = T0[stage]
            last_stage = t0 + NT[stage] == TILES

            def body(i, last):
                for j in range(4):
                    for q in range(per):
                        r = j * per + q
                        dve.wait_ge(tile_done, i * (4 * per) + (t0 + r + 1))
                        if not (last and r >= 4 * per - 2):
                            split_tile(dve, (r + 2) % 4, i * per + ((t0 + r + 2) // 4))
                    nc.vector.tensor_tensor(chunk(h, i * 4 + j), chunk(h, i * 4 + j), view(acc[j % 2][:]),
                                            ALU.add).then_inc(acc_free[j % 2], 1)

            if last_stage:
                body(0, False)
                body(1, True)
            else:
                with dve.Fori(0, 2) as i:
                    body(i, False)

        def act_residual(act, stage, n):
            act_zero_square(act, n)
            with act.Fori(0, 2) as i:
                for j in range(4):
                    act.wait_ge(acc_free[j % 2], freed(O0[stage] + j, i, 2))
                    act_square(act, n, i * 4 + j, j)

        used[0] = base
        ghi = at("ghi", [P, FT, S], F32R)
        glo = at("glo", [P, FT, S], F32R)
        upad = at("upad", [P, 2 + S])
        cw = at("cw", [P, 2, 4, FT])
        c0 = at("c0", [P, S])
        c1 = at("c1", [P, S])
        c2 = at("c2", [P, S])
        gate = at("gate", [P, S])
        gf = at("gf", [P, S])
        cw_landed = sem("cw_landed")
        pad_zero = sem("pad_zero")
        u_copied = sem("u_copied")
        conv1 = sem("conv1")
        conv2 = sem("conv2")
        gated = sem("gated")
        g_ready = sem("g_ready")
        g_lo = sem("g_lo")

        def pe_ffn(pe, layer):
            pe_normed(pe, ORDER[(N_FFN0, N_FFN1)[layer]])
            products_feature_major(pe, f"up{layer}", 0, 2 * FT)
            pe.wait_ge(g_lo, FT * (layer + 1))
            third = FT - 2 * KC
            rhs = [(lambda k, q=q: ghi[:, q * KC + k, :], lambda k, q=q: glo[:, q * KC + k, :]) for q in range(3)]
            after = ORDER[(N_FFN0, N_FFN1)[layer]] + 1
            pe_residual(pe, f"down{layer}", after if after < len(norms) else None, 3, rhs, (KC, KC, third))

        def act_ffn(act, layer):
            stage = f"up{layer}"
            o0, f0 = O0[stage], FT * layer
            act.dma_start(cw[:], A["conv"]).then_inc(cw_landed, 16)
            act.wait_ge(cw_landed, 16 * (layer + 1))
            with act.Fori(0, FT // 2) as i:
                for j in range(2):
                    t = T0[stage] + 2 * j
                    act.wait_ge(tile_done, i * 4 + (t + 1))
                    act.wait_ge(conv2, i * 2 + (f0 + j + 1))
                    nc.scalar.activation(upad[:, 2:], acc[0][:], ACT.Copy).then_inc(u_copied, 1)
                    nc.scalar.activation(c0[:], acc[0][:], ACT.Identity, bias=cw[:, layer, 3, ds(i * 2 + j, 1)],
                                         scale=cw[:, layer, 2, ds(i * 2 + j, 1)]).then_inc(acc_free[0], 1)
                    act.wait_ge(conv2, i * 2 + (f0 + j + 2))
                    nc.scalar.activation(gate[:], c2[:], ACT.Silu).then_inc(gated, 1)
                    act.wait_ge(acc_free[1], i * 2 + ((o0 + 2 * j + 1) // 2 + 2))
                    nc.scalar.activation(chunk(ghi, i * 2 + j), gf[:], ACT.Copy).then_inc(g_ready, 1)

        def dve_ffn(dve, layer):
            stage = f"up{layer}"
            t0, f0 = T0[stage], FT * layer
            nc.vector.memset(upad[:, 0:2], 0.0).then_inc(pad_zero, 1)
            dve.wait_ge(cw_landed, 16 * (layer + 1))
            dve.wait_ge(pad_zero, layer + 1)
            with dve.Fori(0, FT // 2) as i:
                for j in range(2):
                    t = t0 + 2 * j
                    dve.wait_ge(tile_done, i * 4 + (t + 1))
                    split_tile(dve, (2 * j + 2) % 4, i + (t + 2) // 4)
                    dve.wait_ge(u_copied, i * 2 + (f0 + j + 1))
                    dve.wait_ge(acc_free[0], freed(O0[stage] + 2 * j, i, 2))
                    nc.vector.scalar_tensor_tensor(c1[:], upad[:, 1:1 + S], cw[:, layer, 1, ds(i * 2 + j, 1)], c0[:],
                                                   ALU.mult, ALU.add).then_inc(conv1, 1)
                    dve.wait_ge(conv1, i * 2 + (f0 + j + 1))
                    nc.vector.scalar_tensor_tensor(c2[:], upad[:, 0:S], cw[:, layer, 0, ds(i * 2 + j, 1)], c1[:],
                                                   ALU.mult, ALU.add).then_inc(conv2, 1)
                    dve.wait_ge(tile_done, i * 4 + (t + 2))
                    split_tile(dve, (2 * j + 3) % 4, i + (t + 3) // 4)
                    dve.wait_ge(gated, i * 2 + (f0 + j + 1))
                    nc.vector.tensor_tensor(gf[:], gate[:], acc[1][:], ALU.mult).then_inc(acc_free[1], 1)
                    dve.wait_ge(g_ready, i * 2 + (f0 + j + 1))
                    nc.vector.tensor_tensor(chunk(glo, i * 2 + j), gf[:], chunk(ghi, i * 2 + j).bitcast(F32),
                                            ALU.subtract).then_inc(g_lo, 1)
            dve_residual(dve, f"down{layer}", 3)

        used[0] = base
        ein = at("ein", [P, 28, S])
        etab = at("etab", [P, 3 * P + 2 * S + 4 * S + 4])
        bdiag, later_key, before = (etab[:, j * P:(j + 1) * P] for j in range(3))
        cos_t, sin_t = etab[:, 3 * P:3 * P + S], etab[:, 3 * P + S:3 * P + 2 * S]
        decay = etab[:, 3 * P + 2 * S:3 * P + 6 * S].rearrange("p (r s) -> p r s", r=4)
        e64eps = etab[:, 3 * P + 6 * S:3 * P + 6 * S + 1]
        egain = at("egain", [P, 3])
        swap = at("swap", [P, P])
        qs = at("qs", [P, S])
        ks = at("ks", [P, S])
        vs = at("vs", [P, 4, P])
        esq = at("esq", [P, 2, S])
        er = at("er", [P, 2, S])
        ea = at("ea", [P, 2, S])
        el = at("el", [P, 2, S])
        et = at("et", [P, 2, S])
        esp = at("esp", [P, 4, S])
        ew = at("ew", [P, 4, S])
        e_loaded = sem("e_loaded")
        e_in = sem("e_in")
        e_sqr = sem("e_sqr")
        e_ms = sem("e_ms")
        e_ln = sem("e_ln")
        e_r = sem("e_r")
        e_qkv = sem("e_qkv")
        e_z = sem("e_z")
        e_abs = sem("e_abs")
        e_l = sem("e_l")
        e_sp0 = sem("e_sp0")
        e_sp = sem("e_sp")
        e_t = sem("e_t")
        e_rc = sem("e_rc")
        e_t2 = sem("e_t2")
        e_w0 = sem("e_w0")
        e_w = sem("e_w")
        e_o = sem("e_o")
        e_oh = sem("e_oh")
        e_ol = sem("e_ol")
        STEPS = [(hd, jb) for hd in range(2) for jb in (3, 2, 1, 0)]

        def tile_of(x, i):
            return x[:, ds(i, 1), :].rearrange("p a s -> p (a s)")

        def products_token_major(pe, stage, skip, n):
            t0, o0 = T0[stage] + skip, O0[stage] + skip
            with pe.Fori(0, n // 2) as i:
                for j in range(2):
                    pe.wait_ge(w_lo, i * 2 + (t0 + j + 1))
                    pe.wait_ge(acc_free[j], i + ((o0 + j) // 2 + 1))
                    for b in range(4):
                        to = acc[j][:, b * P:(b + 1) * P]
                        for k in range(KC):
                            x_h, x_l = xh[:, k, b * P:(b + 1) * P], xl[:, k, b * P:(b + 1) * P]
                            w_h, w_l = whi[:, j, k * P:(k + 1) * P], wlo[:, j, k * P:(k + 1) * P]
                            nc.tensor.matmul(to, x_h, w_h, start=k == 0, stop=False)
                            nc.tensor.matmul(to, x_h, w_l, start=False, stop=False)
                            mm = nc.tensor.matmul(to, x_l, w_h, start=False, stop=k == KC - 1)
                    mm.then_inc(tile_done, 1)

        def act_take(act, stage, skip, n, to, index=lambda i, j: i * 2 + j, func=ACT.Copy):
            with act.Fori(0, n // 2) as i:
                for j in range(2):
                    act.wait_ge(tile_done, i * 2 + (T0[stage] + skip + j + 1))
                    nc.scalar.activation(tile_of(to, index(i, j)), acc[j][:], func).then_inc(acc_free[j], 1)

        def nth(i, per, k, seed=0):
            return i * per + (k + 1 + seed)

        def pe_even(pe):
            pe_normed(pe, ORDER[N_MIX0])
            products_feature_major(pe, "even_in", 0, 20)
            products_token_major(pe, "even_in", 20, 8)
            pe.wait_ge(e_loaded, 48)
            with pe.Fori(0, 4) as i:
                for j in range(2):
                    pe.wait_ge(e_sqr, nth(i, 2, j))
                    nc.tensor.matmul(bank[2 + j][:], bdiag, esq[:, j, :], start=True, stop=True).then_inc(e_ms, 1)
                pe.wait_ge(e_qkv, nth(i, 3, 2))

                def logits(s):
                    hd, jb = STEPS[s]
                    if s >= 2:
                        pe.wait_ge(e_t, nth(i, 8, s - 2))
                    nc.tensor.matmul(bank[2 + s % 2][:, 0:S - jb * P], ks[64 * hd:64 * hd + 64, jb * P:(jb + 1) * P],
                                     qs[64 * hd:64 * hd + 64, jb * P:S], start=True, stop=True).then_inc(e_z, 1)

                def later_sums(s):
                    hd, jb = STEPS[s]
                    pe.wait_ge(e_sp, nth(i, 8, s))
                    if s >= 2:
                        pe.wait_ge(e_t2, nth(i, 8, s - 2))
                    to = bank[4 + s % 2]
                    mm = nc.tensor.matmul(to[:, 0:S - jb * P], later_key, esp[:, jb, 0:S - jb * P],
                                          start=True, stop=jb == 3)
                    for b in range(jb + 1, 4):
                        mm = nc.tensor.matmul(to[:, (b - jb) * P:S - jb * P], ones, esp[:, b, 0:S - b * P],
                                              start=False, stop=b == 3)
                    mm.then_inc(e_rc, 1)

                def outputs(hd):
                    pe.wait_ge(e_w, nth(i, 8, 4 * hd + 3))
                    if hd == 0:
                        pe.wait_ge(e_ol, nth(i, 1, -1, 1))
                    for jb in range(4):
                        mm = nc.tensor.matmul(bank[6][64 * hd:64 * hd + 64, jb * P:S], vs[:, jb, 64 * hd:64 * hd + 64],
                                              ew[:, jb, 0:S - jb * P], start=jb == 0, stop=jb == 3)
                    mm.then_inc(e_o, 1)

                logits(0)
                logits(1)
                for s in range(8):
                    later_sums(s)
                    if s + 2 < 8:
                        logits(s + 2)
                    if s == 5:
                        outputs(0)
                outputs(1)
            pe_retention(pe)

        def act_even(act):
            act.dma_start(etab[:], A["even_tables"]).then_inc(e_loaded, 16)
            act.dma_start(egain[:], A["even_gains"]).then_inc(e_loaded, 16)
            act.dma_start(swap[:], A["swap"]).then_inc(e_loaded, 16)
            act_take(act, "even_in", 0, 16, ein)
            act_take(act, "even_in", 16, 4, ein, lambda i, j: i * 2 + (16 + j), ACT.Silu)
            act_take(act, "even_in", 20, 8, ein, lambda i, j: i * 2 + (20 + j))
            act.preload_act_table_set(LOG_EXP)
            act.wait_ge(e_loaded, 48)
            act.wait_ge(acc_free[1], freed(O0["even_in"] + 27))
            act.wait_ge(acc_free[0], freed(O0["even_in"] + 26))
            with act.Fori(0, 4) as i:
                for j in range(2):
                    nc.scalar.activation(esq[:, j, :], tile_of(ein, i + 4 * j), ACT.Square).then_inc(e_sqr, 1)
                for j in range(2):
                    act.wait_ge(e_ms, nth(i, 2, j))
                    nc.scalar.activation(er[:, j, :], bank[2 + j][:], ACT.Ln, bias=(e64eps, epsc)[j],
                                         scale=(64.0, 1.0)[j]).then_inc(e_ln, 1)
                    act.wait_ge(e_ln, nth(i, 2, j))
                    nc.scalar.activation(er[:, j, :], er[:, j, :], ACT.Exp, scale=-0.5).then_inc(e_r, 1)

                def soft(s):
                    w = S - STEPS[s][1] * P
                    act.wait_ge(e_z, nth(i, 8, s))
                    if s >= 2:
                        act.wait_ge(e_t, nth(i, 8, s - 2))
                    nc.scalar.activation(ea[:, s % 2, 0:w], bank[2 + s % 2][:, 0:w], ACT.Abs).then_inc(e_abs, 1)
                    act.wait_ge(e_abs, nth(i, 16, 2 * s))
                    nc.scalar.activation(ea[:, s % 2, 0:w], ea[:, s % 2, 0:w], ACT.Exp, scale=-1.0).then_inc(e_abs, 1)
                    act.wait_ge(e_abs, nth(i, 16, 2 * s + 1))
                    nc.scalar.activation(el[:, s % 2, 0:w], ea[:, s % 2, 0:w], ACT.Ln, bias=ones[:, 0:1]).then_inc(e_l, 1)

                def weight(s):
                    hd, jb = STEPS[s]
                    act.wait_ge(e_t2, nth(i, 8, s))
                    if hd == 0:
                        act.wait_ge(e_o, nth(i, 2, -1, 1))
                    else:
                        act.wait_ge(e_o, nth(i, 2, 0, 1))
                    nc.scalar.activation(ew[:, jb, 0:S - jb * P], et[:, s % 2, 0:S - jb * P], ACT.Exp).then_inc(e_w0, 1)

                soft(0)
                for s in range(9):
                    if s + 1 < 8:
                        soft(s + 1)
                    if s >= 1:
                        weight(s - 1)
                act.wait_ge(e_o, nth(i, 2, 1, 1))
                nc.scalar.activation(tile_of(xh, i), bank[6][:], ACT.Copy).then_inc(e_oh, 1)
            act_retention(act)

        def dve_even(dve):
            splits_only(dve, "even_in", 0, 28)
            dve.wait_ge(e_loaded, 48)
            dve.wait_ge(acc_free[1], freed(O0["even_in"] + 27))
            dve.wait_ge(acc_free[0], freed(O0["even_in"] + 26))
            with dve.Fori(0, 4) as i:
                dve.wait_ge(e_o, nth(i, 2, -1, 1))
                nc.vector.tensor_copy(vs[:].rearrange("p b f -> p (b f)"), tile_of(ein, i + 20)).then_inc(e_qkv, 1)
                for j in range(2):
                    dve.wait_ge(e_r, nth(i, 2, j))
                    nc.vector.scalar_tensor_tensor((qs, ks)[j][:], tile_of(ein, i + 4 * j), egain[:, j:j + 1],
                                                   er[:, j, :], ALU.mult, ALU.mult).then_inc(e_qkv, 1)

                def soft(s):
                    hd, jb = STEPS[s]
                    w = S - jb * P
                    dve.wait_ge(e_l, nth(i, 8, s))
                    if hd == 1 and jb == 3:
                        dve.wait_ge(e_rc, nth(i, 8, 3))
                    z = bank[2 + s % 2][:, 0:w]
                    nc.vector.scalar_tensor_tensor(esp[:, jb, 0:w], z, 0.0, el[:, s % 2, 0:w],
                                                   ALU.max, ALU.add).then_inc(e_sp0, 1)
                    dve.wait_ge(e_sp0, nth(i, 8, s))
                    nc.vector.tensor_tensor(esp[:, jb, 0:P], esp[:, jb, 0:P], before, ALU.mult).then_inc(e_sp, 1)
                    if s >= 2:
                        dve.wait_ge(e_w0, nth(i, 8, s - 2))
                    nc.vector.scalar_tensor_tensor(et[:, s % 2, 0:w], z, 0.0, el[:, s % 2, 0:w],
                                                   ALU.min, ALU.subtract).then_inc(e_t, 1)

                def log_weight(s):
                    w = S - STEPS[s][1] * P
                    dve.wait_ge(e_rc, nth(i, 8, s))
                    dve.wait_ge(e_t, nth(i, 8, s))
                    nc.vector.tensor_tensor(et[:, s % 2, 0:w], et[:, s % 2, 0:w], bank[4 + s % 2][:, 0:w],
                                            ALU.subtract).then_inc(e_t2, 1)

                def mask_weight(s):
                    jb = STEPS[s][1]
                    dve.wait_ge(e_w0, nth(i, 8, s))
                    nc.vector.tensor_tensor(ew[:, jb, 0:P], ew[:, jb, 0:P], before, ALU.mult).then_inc(e_w, 1)

                for s in range(10):
                    if s < 8:
                        soft(s)
                    if 1 <= s < 9:
                        log_weight(s - 1)
                    if s >= 2:
                        mask_weight(s - 2)
                dve.wait_ge(e_oh, nth(i, 1, 0))
                nc.vector.tensor_tensor(tile_of(xl, i), bank[6][:], tile_of(xh, i).bitcast(F32),
                                        ALU.subtract).then_inc(e_ol, 1)
            dve_retention(dve)

        r_sq = sem("r_sq")
        r_rot = sem("r_rot")
        r_part = sem("r_part")
        r_qkv = sem("r_qkv")
        r_s = sem("r_s")
        r_w = sem("r_w")
        r_o = sem("r_o")
        r_ms = sem("r_ms")
        r_ln = sem("r_ln")
        r_r = sem("r_r")
        r_m = sem("r_m")
        r_mix = sem("r_mix")
        r_hi = sem("r_hi")
        r_lo = sem("r_lo")

        def pe_retention(pe):
            with pe.Fori(0, 4) as i:
                for j in range(2):
                    nc.tensor.matmul(bank[2 + j][:], swap[:], tile_of(ein, i + (8 + 4 * j)),
                                     start=True, stop=True).then_inc(r_rot, 1)
                pe.wait_ge(r_qkv, nth(i, 3, 2))
                for jb in range(4):
                    if jb >= 2:
                        pe.wait_ge(r_w, nth(i, 4, jb - 2))
                    nc.tensor.matmul(bank[2 + jb % 2][:, 0:S - jb * P], ks[:, jb * P:(jb + 1) * P], qs[:, jb * P:S],
                                     start=True, stop=True).then_inc(r_s, 1)
                for jb in range(4):
                    pe.wait_ge(r_w, nth(i, 4, jb))
                    mm = nc.tensor.matmul(bank[6][:, jb * P:S], vs[:, jb, :], ew[:, jb, 0:S - jb * P],
                                          start=jb == 0, stop=jb == 3)
                mm.then_inc(r_o, 1)
                pe.wait_ge(r_sq, nth(i, 1, 0))
                nc.tensor.matmul(bank[4][:], ones, esq[:, 0, :], start=True, stop=True).then_inc(r_ms, 1)
                pe.wait_ge(r_m, nth(i, 1, 0))

        def act_retention(act):
            with act.Fori(0, 4) as i:
                act.wait_ge(r_o, nth(i, 1, 0, 1))
                nc.scalar.activation(esq[:, 0, :], bank[6][:], ACT.Square).then_inc(r_sq, 1)
                act.wait_ge(r_ms, nth(i, 1, 0))
                nc.scalar.activation(er[:, 0, :], bank[4][:], ACT.Ln, bias=epsc, scale=1.0 / P).then_inc(r_ln, 1)
                act.wait_ge(r_ln, nth(i, 1, 0))
                nc.scalar.activation(er[:, 0, :], er[:, 0, :], ACT.Exp, scale=-0.5).then_inc(r_r, 1)
                act.wait_ge(r_mix, nth(i, 1, 0, 1))
                nc.scalar.activation(tile_of(xh, i + 4), ea[:, 0, :], ACT.Copy).then_inc(r_hi, 1)

        def dve_retention(dve):
            with dve.Fori(0, 4) as i:
                dve.wait_ge(r_o, nth(i, 1, -1, 1))
                nc.vector.tensor_copy(vs[:].rearrange("p b f -> p (b f)"), tile_of(ein, i + 24)).then_inc(r_qkv, 1)
                for j in range(2):
                    nc.vector.tensor_tensor(et[:, j, :], tile_of(ein, i + (8 + 4 * j)), cos_t, ALU.mult).then_inc(r_part, 1)
                for j in range(2):
                    dve.wait_ge(r_rot, nth(i, 2, j))
                    nc.vector.tensor_tensor(el[:, j, :], bank[2 + j][:], sin_t, ALU.mult).then_inc(r_part, 1)
                for j in range(2):
                    dve.wait_ge(r_part, nth(i, 4, 2 + j))
                    nc.vector.tensor_tensor((qs, ks)[j][:], et[:, j, :], el[:, j, :], ALU.add).then_inc(r_qkv, 1)
                for jb in range(4):
                    dve.wait_ge(r_s, nth(i, 4, jb))
                    nc.vector.tensor_tensor(ew[:, jb, 0:S - jb * P], bank[2 + jb % 2][:, 0:S - jb * P],
                                            decay[:, ds(i, 1), 0:S - jb * P].rearrange("p a s -> p (a s)"),
                                            ALU.mult).then_inc(r_w, 1)
                dve.wait_ge(r_r, nth(i, 1, 0))
                nc.vector.scalar_tensor_tensor(et[:, 0, :], bank[6][:], egain[:, 2:3], er[:, 0, :],
                                               ALU.mult, ALU.mult).then_inc(r_m, 1)
                dve.wait_ge(r_m, nth(i, 1, 0))
                nc.vector.tensor_tensor(ea[:, 0, :], et[:, 0, :], tile_of(ein, i + 16), ALU.mult).then_inc(r_mix, 1)
                dve.wait_ge(r_hi, nth(i, 1, 0))
                nc.vector.tensor_tensor(tile_of(xl, i + 4), ea[:, 0, :], tile_of(xh, i + 4).bitcast(F32),
                                        ALU.subtract).then_inc(r_lo, 1)

        used[0] = base
        NW = 32
        nin = at("nin", [P, 20, S])
        used[0] = base
        x2 = [[at(f"x2_{kv}{part}", [P, 4, S + 16], F32R) for part in "hl"] for kv in "kv"]
        used[0] = max(used[0], base + 20 * S * 4)
        work = used[0]
        kvc = [at(f"kvc_{part}", [P, 4, S], F32R) for part in "hl"]
        used[0] = work
        qst = at("qst", [P, S])
        dist = at("dist", [P, 2, S])
        ssb = at("ssb", [P, 2, 2, S])
        prob = at("prob", [P, 2, 2, S])
        probt = at("probt", [P, 2, S])
        nk = at("nk", [P, 4, S])
        ntab = at("ntab", [P, S + 3 * P + 16])
        dist_t, cdist_t = ntab[:, 0:S], ntab[:, S:S + P]
        cmask = ntab[:, S + P:S + 3 * P].rearrange("p (s n) -> p s n", n=NW)
        slopes = ntab[:, S + 3 * P:S + 3 * P + 16]
        wgate = at("wgate", [P, KC, 48])
        w2 = at("w2", [P, 2, 3 * 64])
        pe_in = at("pe_in", [P, 2, 16, 2])
        pe_h = at("pe_h", [P, 2, 16, 2], F32R)
        pe_l = at("pe_l", [P, 2, 16, 2], F32R)
        cbias = at("cbias", [P, 4, 2])
        chid = at("chid", [P, 4, P])
        kcmp = at("kcmp", [P, P])
        vcmp = at("vcmp", [NW, 4, 64])
        gsig = at("gsig", [P, 4, 48])
        csc = at("csc", [P, 8, NW])
        cpr = at("cpr", [P, 8, NW])
        cst = at("cst", [P, 4, 8])
        cpt = at("cpt", [NW, 2, S])
        stat = at("stat", [P, 2, 8])
        oacc = at("oacc", [P, 4, P])
        nmix = at("nmix", [P, S])
        n_loaded = sem("n_loaded")
        n_gmm = sem("n_gmm")
        n_gs = sem("n_gs")
        n_zero = sem("n_zero")
        n_pe = sem("n_pe")
        n_kvh = sem("n_kvh")
        n_x2 = sem("n_x2")
        n_cb = sem("n_cb")
        n_c2 = sem("n_c2")
        n_cc = sem("n_cc")
        n_q = sem("n_q")
        n_dist = sem("n_dist")
        n_cs = sem("n_cs")
        n_c = sem("n_c")
        n_ce = sem("n_ce")
        n_cp = sem("n_cp")
        n_cd = sem("n_cd")
        n_ct = sem("n_ct")
        n_cta = sem("n_cta")
        n_ctv = sem("n_ctv")
        n_co = sem("n_co")
        n_s = sem("n_s")
        n_turn = sem("n_turn")
        n_m = sem("n_m")
        n_nm = sem("n_nm")
        n_e = sem("n_e")
        n_t = sem("n_t")
        n_pa = sem("n_pa")
        n_pv = sem("n_pv")
        n_g0 = sem("n_g0")
        n_cf = sem("n_cf")
        n_o = sem("n_o")
        n_acc = sem("n_acc")
        n_ot = sem("n_ot")
        n_mix = sem("n_mix")
        n_hi = sem("n_hi")
        n_lo = sem("n_lo")
        NSTEP = [(hd, qb) for hd in range(2) for qb in range(4)]

        def nsa_loads(act):
            for to, what in ((ntab, "nsa_tables"), (wgate, "wgate"), (w2, "w2"), (pe_in, "pe")):
                act.dma_start(to[:], A[what]).then_inc(n_loaded, 16)

        def pe_nsa_gate(pe, n):
            pe.wait_ge(n_loaded, 64)
            for m in range(KC):
                pe.wait_ge(norm_f, 8 * n + m + 1)
                for b in range(4):
                    mm = nc.tensor.matmul(bank[2 + b][:, 0:48], xf[:, m % 2, b * P:(b + 1) * P], wgate[:, m, :],
                                          start=m == 0, stop=m == KC - 1)
                mm.then_inc(n_gmm, 1)

        def pe_nsa(pe):
            n = ORDER[N_NSA]
            pe_nsa_gate(pe, n)
            pe_normed(pe, n)
            products_feature_major(pe, "nsa_kv", 0, 8)
            pe.wait_ge(n_x2, 16 * 16)
            pe.wait_ge(n_pe, 2)
            pe.wait_ge(n_gs, 4)
            t0, o0 = T0["cmp"], O0["cmp"]
            for o in range(4):
                kv = o // 2
                for q in range(2):
                    pe.wait_ge(w_lo, t0 + 2 * o + q + 1)
                    if q == 0:
                        pe.wait_ge(acc_free[o % 2], (o0 + o) // 2 + 1)
                    for k in range(KC):
                        lp = q * KC + k
                        first, last = lp == 0, lp == 2 * KC - 1
                        w_h, w_l = whi[:, q, k * P:(k + 1) * P], wlo[:, q, k * P:(k + 1) * P]
                        x_h, x_l = (x2[kv][part][:, :, 2 * lp:2 * lp + 16 * NW - 15:16] for part in range(2))
                        to, tb = acc[o % 2][:, 0:4 * NW], bank[2 + o][:, 0:2]
                        nc.tensor.matmul(to, w_h, x_h, start=first, stop=False)
                        nc.tensor.matmul(to, w_h, x_l, start=False, stop=False)
                        nc.tensor.matmul(to, w_l, x_h, start=False, stop=last)
                        nc.tensor.matmul(tb, w_h, pe_h[:, kv, lp, :], start=first, stop=False)
                        nc.tensor.matmul(tb, w_h, pe_l[:, kv, lp, :], start=False, stop=False)
                        mm = nc.tensor.matmul(tb, w_l, pe_h[:, kv, lp, :], start=False, stop=last)
                    mm.then_inc(tile_done, 1)
            products_feature_major(pe, "nsa_rest", 0, 16)
            products_token_major(pe, "nsa_rest", 16, 4)
            for half in range(2):
                nc.tensor.matmul(bank[2][:, 0:P], w2[:, half, 0:P], chid[:, half, :], start=half == 0, stop=half == 1)
            for g in range(4):
                for half in range(2):
                    mm = nc.tensor.matmul(bank[3][0:NW, g * 64:(g + 1) * 64], chid[:, 2 + half, g * NW:(g + 1) * NW],
                                          w2[:, half, P:P + 64], start=half == 0, stop=half == 1)
            mm.then_inc(n_c2, 1)
            pe.wait_ge(n_cc, 2)
            pe.wait_ge(acc_free[0], freed(O0["nsa_rest"] + 18))
            pe.wait_ge(acc_free[1], freed(O0["nsa_rest"] + 19))
            for j in range(2):
                with pe.Fori(4 * j, 4 * j + 4) as i:
                    pe_nsa_pair(pe, i, j)

        def pe_nsa_pair(pe, i, j):
            pe.wait_ge(n_q, nth(i, 1, 0))
            for hd in range(2):
                b, g = 64 * hd, 2 * j + hd
                for qb in range(4):
                    mm = nc.tensor.matmul(bank[hd][:, qb * NW:(qb + 1) * NW], qst[b:b + 64, qb * P:(qb + 1) * P],
                                          kcmp[b:b + 64, g * NW:(g + 1) * NW], start=True, stop=True)
            mm.then_inc(n_cs, 1)

            def scores(s):
                hd, qb = NSTEP[s]
                b, w = 64 * hd, (qb + 1) * P
                if s >= 2:
                    pe.wait_ge(n_nm, nth(i, 8, s - 2))
                for br in range(2):
                    mm = nc.tensor.matmul(bank[2 + 2 * br + s % 2][:, 0:w], qst[b:b + 64, qb * P:(qb + 1) * P],
                                          nk[b:b + 64, 2 * br + j, 0:w], start=True, stop=True)
                mm.then_inc(n_s, 1)

            scores(0)
            scores(1)
            pe.wait_ge(n_cp, nth(i, 1, 0))
            for s in range(8):
                mm = nc.tensor.transpose(bank[6 + s // 4][0:NW, (s % 4) * P:(s % 4 + 1) * P], cpr[:, s, :], ident)
            mm.then_inc(n_ct, 1)
            pe.wait_ge(n_cta, nth(i, 1, 0))
            pe.wait_ge(n_ctv, nth(i, 1, 0))
            for s, (hd, qb) in enumerate(NSTEP):
                mm = nc.tensor.matmul(bank[0][:, s * 64:(s + 1) * 64], cpt[:, hd, qb * P:(qb + 1) * P],
                                      vcmp[:, 2 * j + hd, :], start=True, stop=True)
            mm.then_inc(n_co, 1)
            for s, (hd, qb) in enumerate(NSTEP):
                pe.wait_ge(n_e, nth(i, 16, 2 * s + 1))
                if s:
                    pe.wait_ge(n_pa, nth(i, 8, s - 1))
                    pe.wait_ge(n_pv, nth(i, 8, s - 1))
                for br in range(2):
                    for kb in range(qb + 1):
                        mm = nc.tensor.transpose(bank[6 + br][:, kb * P:(kb + 1) * P],
                                                 prob[:, s % 2, br, kb * P:(kb + 1) * P], ident)
                mm.then_inc(n_t, 1)
                if s + 2 < 8:
                    scores(s + 2)
                pe.wait_ge(n_pa, nth(i, 8, s))
                pe.wait_ge(n_pv, nth(i, 8, s))
                pe.wait_ge(n_acc, nth(i, 17, 2 * (s - 2) + 2 if s >= 2 else 0))
                for br in range(2):
                    for kb in range(qb + 1):
                        mm = nc.tensor.matmul(bank[s % 2][:, br * 64:(br + 1) * 64], probt[:, br, kb * P:(kb + 1) * P],
                                              nin[:, 16 + 2 * br + j, kb * P + 64 * hd:kb * P + 64 * hd + 64],
                                              start=kb == 0, stop=kb == qb)
                mm.then_inc(n_o, 1)
            pe.wait_ge(n_acc, nth(i, 17, 16))
            for qb in range(4):
                mm = nc.tensor.transpose(bank[6][:, qb * P:(qb + 1) * P], oacc[:, qb, :], ident)
            mm.then_inc(n_ot, 1)
            pe.wait_ge(n_mix, nth(i, 1, 0))

        def act_nsa(act):
            T = T0["nsa_kv"]
            act.wait_ge(n_gmm, KC + 2)
            for b in range(4):
                nc.scalar.activation(gsig[:, b, :], bank[2 + b][:, 0:48], ACT.Sigmoid).then_inc(n_gs, 1)
            for u in range(4):
                act.wait_ge(tile_done, T + u + 1)
                nc.scalar.activation(kvc[0][:, u, :], acc[u % 2][:], ACT.Copy).then_inc(n_kvh, 1)
            act.wait_ge(n_zero, 4)
            for kv in range(2):
                act.wait_ge(acc_free[0], freed(O0["nsa_kv"] + 2 * kv))
                act.wait_ge(acc_free[1], freed(O0["nsa_kv"] + 2 * kv + 1))
                for part in range(2):
                    for nxt in range(2):
                        for odd in range(2):
                            act.dma_start(x2[kv][part][64 * nxt:64 * nxt + 64, odd:4:2, 0:S - nxt].bitcast(F32),
                                          kvc[part][64 * odd:64 * odd + 64, 2 * kv:2 * kv + 2, nxt:S].bitcast(F32))\
                               .then_inc(n_x2, 16)
            for u in range(4):
                act.wait_ge(tile_done, T + 4 + u + 1)
                nc.scalar.activation(nk[:, u, :], acc[u % 2][:], ACT.Copy).then_inc(acc_free[u % 2], 1)
            for o in range(4):
                act.wait_ge(tile_done, T0["cmp"] + 2 * o + 2)
                nc.scalar.activation(cbias[:, o, :], bank[2 + o][:, 0:2], ACT.Copy).then_inc(n_cb, 1)
                act.wait_ge(n_cb, o + 1)
                nc.scalar.activation(chid[:, o, :], acc[o % 2][:, 0:P], ACT.Silu,
                                     bias=cbias[:, o, 0:1]).then_inc(acc_free[o % 2], 1)
            act_take(act, "nsa_rest", 0, 8, nin)
            act_take(act, "nsa_rest", 8, 8, nin, lambda i, j: i * 2 + (8 + j), ACT.Silu)
            act_take(act, "nsa_rest", 16, 4, nin, lambda i, j: i * 2 + (16 + j))
            act.wait_ge(n_c2, 1)
            nc.scalar.activation(kcmp[:], bank[2][:, 0:P], ACT.Copy).then_inc(n_cc, 1)
            nc.scalar.activation(vcmp[:].rearrange("n g d -> n (g d)"), bank[3][0:NW, 0:4 * 64],
                                 ACT.Copy).then_inc(n_cc, 1)
            act.preload_act_table_set(LOG_EXP)
            for j in range(2):
                with act.Fori(4 * j, 4 * j + 4) as i:
                    act_nsa_pair(act, i)

        def act_nsa_pair(act, i):
            act.wait_ge(n_lo, nth(i, 1, -1, 1))
            for hd in range(2):
                nc.scalar.activation(dist[:, hd, :], dist_t, ACT.Copy,
                                     scale=slopes[:, ds(i * 2 + hd, 1)]).then_inc(n_dist, 1)
            act.wait_ge(n_c, nth(i, 4, 3))
            nc.scalar.activation(cpr[:], csc[:], ACT.Exp).then_inc(n_ce, 1)
            act.wait_ge(n_ct, nth(i, 1, 0))
            nc.scalar.activation(cpt[:, 0, :], bank[6][0:NW, :], ACT.Copy).then_inc(n_cta, 1)

            def exps(s):
                w = (NSTEP[s][1] + 1) * P
                act.wait_ge(n_nm, nth(i, 8, s))
                if s >= 2:
                    act.wait_ge(n_t, nth(i, 8, s - 2))
                    act.wait_ge(n_cf, nth(i, 8, s - 2))
                for br in range(2):
                    nc.scalar.activation(prob[:, s % 2, br, 0:w], ssb[:, s % 2, br, 0:w], ACT.Exp,
                                         bias=stat[:, s % 2, 2 + br:3 + br],
                                         accum_out=stat[:, s % 2, 4 + br:5 + br]).then_inc(n_e, 1)

            exps(0)
            for s in range(8):
                if s + 1 < 8:
                    exps(s + 1)
                w = (NSTEP[s][1] + 1) * P
                act.wait_ge(n_t, nth(i, 8, s))
                if s:
                    act.wait_ge(n_o, nth(i, 8, s - 1))
                nc.scalar.activation(probt[:, 1, 0:w], bank[7][:, 0:w], ACT.Copy).then_inc(n_pa, 1)
            act.wait_ge(n_mix, nth(i, 1, 0))
            nc.scalar.activation(tile_of(xh, i), nmix[:], ACT.Copy).then_inc(n_hi, 1)

        def dve_nsa(dve):
            T = T0["nsa_kv"]
            dve.wait_ge(n_loaded, 64)
            for kv in range(2):
                for part in range(2):
                    nc.vector.memset(x2[kv][part][:, :, S - 1:S + 16].bitcast(F32), 0.0).then_inc(n_zero, 1)
            nc.vector.tensor_copy(pe_h[:], pe_in[:]).then_inc(n_pe, 1)
            dve.wait_ge(n_pe, 1)
            nc.vector.tensor_tensor(pe_l[:], pe_in[:], pe_h[:].bitcast(F32), ALU.subtract).then_inc(n_pe, 1)
            for u in range(8):
                dve.wait_ge(tile_done, T + u + 1)
                split_tile(dve, (u + 2) % 4, (T + u + 2) // 4)
                if u < 4:
                    dve.wait_ge(n_kvh, u + 1)
                    nc.vector.tensor_tensor(kvc[1][:, u, :], acc[u % 2][:], kvc[0][:, u, :].bitcast(F32),
                                            ALU.subtract).then_inc(acc_free[u % 2], 1)
            splits_only(dve, "cmp", 0, 8)
            splits_only(dve, "nsa_rest", 0, 20)
            dve.wait_ge(acc_free[0], freed(O0["nsa_rest"] + 18))
            dve.wait_ge(acc_free[1], freed(O0["nsa_rest"] + 19))
            for j in range(2):
                with dve.Fori(4 * j, 4 * j + 4) as i:
                    dve_nsa_pair(dve, i)

        def dve_nsa_pair(dve, i):
            dve.wait_ge(n_lo, nth(i, 1, -1, 1))
            nc.vector.tensor_scalar(qst[:], tile_of(nin, i), 0.125, None, ALU.mult).then_inc(n_q, 1)
            dve.wait_ge(n_cs, nth(i, 1, 0))
            for hd in range(2):
                nc.vector.scalar_tensor_tensor(csc[:, 4 * hd:4 * hd + 4, :].rearrange("p a n -> p (a n)"), cdist_t,
                                               slopes[:, ds(i * 2 + hd, 1)], bank[hd][:, 0:P],
                                               ALU.mult, ALU.add).then_inc(n_c, 1)
            dve.wait_ge(n_c, nth(i, 4, 1))
            nc.vector.tensor_reduce(cst[:, 0, :], csc[:], AX.X, ALU.max).then_inc(n_c, 1)
            dve.wait_ge(n_c, nth(i, 4, 2))
            nc.vector.tensor_tensor(csc[:], csc[:], cst[:, 0, :].unsqueeze(2).broadcast_to([P, 8, NW]),
                                    ALU.subtract).then_inc(n_c, 1)

            def maxima(s):
                hd, qb = NSTEP[s]
                w = (qb + 1) * P
                dve.wait_ge(n_s, nth(i, 8, s))
                if s == 0:
                    dve.wait_ge(n_dist, nth(i, 2, 1))
                else:
                    dve.wait_ge(n_e, nth(i, 16, 2 * (s - 2) + 1)) if s >= 2 else None
                nc.vector.memset(seedt[:, 32:33], 0.0).then_inc(n_turn, 1)
                for br in range(2):
                    nc.vector.tensor_tensor_reduce(ssb[:, s % 2, br, 0:w], bank[2 + 2 * br + s % 2][:, 0:w],
                                                   dist[:, hd, (3 - qb) * P:S], 1.0, -3e38, ALU.add, ALU.max,
                                                   stat[:, s % 2, br:br + 1]).then_inc(n_m, 1)
                dve.wait_ge(n_m, nth(i, 16, 2 * s + 1))
                nc.vector.tensor_scalar(stat[:, s % 2, 2:4], stat[:, s % 2, 0:2], -1.0, None, ALU.mult).then_inc(n_nm, 1)

            maxima(0)
            dve.wait_ge(n_ce, nth(i, 1, 0))
            nc.vector.tensor_tensor(cpr[:], cpr[:], cmask, ALU.mult).then_inc(n_cp, 1)
            dve.wait_ge(n_cp, nth(i, 1, 0))
            nc.vector.tensor_reduce(cst[:, 1, :], cpr[:], AX.X, ALU.add).then_inc(n_cd, 1)
            dve.wait_ge(n_cd, nth(i, 4, 0))
            nc.vector.tensor_scalar(cst[:, 1, :], cst[:, 1, :], 1e-30, None, ALU.max).then_inc(n_cd, 1)
            dve.wait_ge(n_cd, nth(i, 4, 1))
            nc.vector.reciprocal(cst[:, 1, :], cst[:, 1, :]).then_inc(n_cd, 1)
            dve.wait_ge(n_cd, nth(i, 4, 2))
            nc.vector.tensor_tensor(cst[:, 2, :].rearrange("p (h b) -> p h b", h=2),
                                    gsig[:, :, ds(i * 6, 6)].rearrange("p b (h k) -> p h b k", h=2)[:, :, :, 0],
                                    cst[:, 1, :].rearrange("p (h b) -> p h b", h=2), ALU.mult).then_inc(n_cd, 1)
            dve.wait_ge(n_ct, nth(i, 1, 0))
            nc.vector.tensor_copy(cpt[:, 1, :], bank[7][0:NW, :]).then_inc(n_ctv, 1)
            maxima(1)
            dve.wait_ge(n_co, nth(i, 1, 0))
            dve.wait_ge(n_cd, nth(i, 4, 3))
            nc.vector.tensor_tensor(oacc[:].rearrange("p b (h d) -> p h b d", h=2),
                                    bank[0][:].rearrange("p (h b d) -> p h b d", h=2, b=4),
                                    cst[:, 2, :].rearrange("p (h b) -> p h b", h=2).unsqueeze(3)
                                    .broadcast_to([P, 2, 4, 64]), ALU.mult).then_inc(n_acc, 1)

            def add(s):
                hd, qb = NSTEP[s]
                dve.wait_ge(n_o, nth(i, 8, s))
                to = oacc[:, qb, 64 * hd:64 * hd + 64]
                dve.wait_ge(n_cf, nth(i, 8, s))
                for br in range(2):
                    dve.wait_ge(n_acc, nth(i, 17, 2 * s + br))
                    nc.vector.scalar_tensor_tensor(to, bank[s % 2][:, br * 64:(br + 1) * 64],
                                                   stat[:, s % 2, 6 + br:7 + br], to,
                                                   ALU.mult, ALU.add).then_inc(n_acc, 1)

            for s in range(8):
                if 2 <= s + 1 < 8:
                    maxima(s + 1)
                hd, qb = NSTEP[s]
                w = (qb + 1) * P
                dve.wait_ge(n_t, nth(i, 8, s))
                if s:
                    dve.wait_ge(n_o, nth(i, 8, s - 1))
                nc.vector.tensor_copy(probt[:, 0, 0:w], bank[6][:, 0:w]).then_inc(n_pv, 1)
                if s:
                    add(s - 1)
                dve.wait_ge(n_e, nth(i, 16, 2 * s + 1))
                nc.vector.tensor_scalar(stat[:, s % 2, 4:6], stat[:, s % 2, 4:6], 1e-30, None, ALU.max).then_inc(n_g0, 1)
                dve.wait_ge(n_g0, nth(i, 16, 2 * s))
                nc.vector.reciprocal(stat[:, s % 2, 4:6], stat[:, s % 2, 4:6]).then_inc(n_g0, 1)
                dve.wait_ge(n_g0, nth(i, 16, 2 * s + 1))
                nc.vector.tensor_tensor(stat[:, s % 2, 6:8], gsig[:, qb, ds(i * 6 + (3 * hd + 1), 2)],
                                        stat[:, s % 2, 4:6], ALU.mult).then_inc(n_cf, 1)
            add(7)
            dve.wait_ge(n_ot, nth(i, 1, 0))
            nc.vector.tensor_tensor(nmix[:], bank[6][:], tile_of(nin, i + 8), ALU.mult).then_inc(n_mix, 1)
            dve.wait_ge(n_hi, nth(i, 1, 0))
            nc.vector.tensor_tensor(tile_of(xl, i), nmix[:], tile_of(xh, i).bitcast(F32), ALU.subtract).then_inc(n_lo, 1)

        used[0] = base
        CH, NCH = 64, S // 64
        oin = at("oin", [P, 24, S])
        otab = at("otab", [P, 2 * S])
        restart, causal = otab[:, 0:S], otab[:, S:2 * S]
        wga = at("wga", [P, KC, 16])
        walpha = at("walpha", [16, 4 * P])
        obias = at("obias", [P, 6])
        gas = at("gas", [16, S])
        oa = at("oa", [P, S])
        omin = at("omin", [P, S])
        cum = at("cum", [P, 4, S])
        oe = at("oe", [P, 3, S])
        qt = at("qt", [P, S])
        kt = at("kt", [P, S])
        kd = at("kd", [P, S])
        kdt = at("kdt", [P, S])
        vo = at("vo", [P, 2, S])
        att = at("att", [P, S])
        state = at("state", [P, NCH - 1, 2 * P])
        osq = at("osq", [P, 2, S])
        orr = at("orr", [P, S])
        omix = at("omix", [P, 2, S])
        o_loaded = sem("o_loaded")
        o_gmm = sem("o_gmm")
        o_ga = sem("o_ga")
        o_al = sem("o_al")
        o_ab = sem("o_ab")
        o_l = sem("o_l")
        o_mn = sem("o_mn")
        o_cum = sem("o_cum")
        o_df = sem("o_df")
        o_e = sem("o_e")
        o_v = sem("o_v")
        o_qk = sem("o_qk")
        o_at = sem("o_at")
        o_am = sem("o_am")
        o_tr = sem("o_tr")
        o_kt = sem("o_kt")
        o_c = sem("o_c")
        o_s = sem("o_s")
        o_o = sem("o_o")
        o_sq = sem("o_sq")
        o_ms = sem("o_ms")
        o_ln = sem("o_ln")
        o_r = sem("o_r")
        o_m = sem("o_m")
        o_mix = sem("o_mix")
        o_hi = sem("o_hi")
        o_lo = sem("o_lo")

        def of_chunk(c):
            half = (c // 2) % 2
            return bank[2 + 2 * (c % 2) + c // 4][:, half * 2 * P:(half + 1) * 2 * P]

        def pe_odd_gate(pe, n):
            pe.wait_ge(o_loaded, 64)
            for m in range(KC):
                pe.wait_ge(norm_f, 8 * n + m + 1)
                nc.tensor.matmul(bank[2][0:16, :], wga[:, m, :], xf[:, m % 2, :], start=m == 0,
                                 stop=m == KC - 1).then_inc(o_gmm, 1)

        def pe_odd(pe):
            pe_odd_gate(pe, ORDER[N_MIX1])
            pe_normed(pe, ORDER[N_MIX1])
            products_feature_major(pe, "odd_in", 0, 16)
            products_token_major(pe, "odd_in", 16, 8)
            pe.wait_ge(o_ga, 1)
            for hd in range(4):
                nc.tensor.matmul(bank[3 + hd][:], walpha[:, hd * P:(hd + 1) * P], gas[:],
                                 start=True, stop=True).then_inc(o_al, 1)
            pe.wait_ge(o_mn, 8)
            pe.wait_ge(acc_free[0], freed(O0["odd_in"] + 22))
            pe.wait_ge(acc_free[1], freed(O0["odd_in"] + 23))
            with pe.Fori(0, 4) as i:
                pe.wait_ge(o_qk, nth(i, 3, 1))
                for b in range(4):
                    mm = nc.tensor.matmul(bank[6][:, b * P:(b + 1) * P], kt[:, b * P:(b + 1) * P],
                                          qt[:, b * P:(b + 1) * P], start=True, stop=True)
                mm.then_inc(o_at, 1)
                pe.wait_ge(o_qk, nth(i, 3, 2))
                for b in range(4):
                    mm = nc.tensor.transpose(bank[5][:, b * P:(b + 1) * P], kd[:, b * P:(b + 1) * P], ident)
                mm.then_inc(o_tr, 1)
                pe.wait_ge(o_kt, nth(i, 1, 0))
                pe.wait_ge(o_v, nth(i, 2, 1))
                for c in range(NCH - 1):
                    b, tb = 64 * (c % 2), c // 2
                    nc.tensor.matmul(of_chunk(c),
                                     kdt[b:b + 64, tb * P:(tb + 1) * P], vo[b:b + 64, :, tb * P:(tb + 1) * P],
                                     start=True, stop=True).then_inc(o_c, 1)
                pe.wait_ge(o_am, nth(i, 1, 0, 1))
                pe.wait_ge(o_lo, nth(i, 2, -1, 1))
                for b in range(4):
                    for e in range(2):
                        nc.tensor.matmul(acc[e][:, b * P:(b + 1) * P], vo[:, e, b * P:(b + 1) * P],
                                         att[:, b * P:(b + 1) * P], start=True, stop=False)
                    for c in (2 * b, 2 * b + 1):
                        if c:
                            pe.wait_ge(o_s, nth(i, 7, c - 1))
                            for e in range(2):
                                mm = nc.tensor.matmul(acc[e][:, c * CH:(c + 1) * CH], state[:, c - 1, e * P:(e + 1) * P],
                                                      qt[:, c * CH:(c + 1) * CH], start=False, stop=c % 2 == 1)
                mm.then_inc(o_o, 1)
                for e in range(2):
                    pe.wait_ge(o_sq, nth(i, 2, e))
                    mm = nc.tensor.matmul(bank[4][:], ones, osq[:, e, :], start=e == 0, stop=e == 1)
                mm.then_inc(o_ms, 1)

        def act_odd(act):
            n = ORDER[N_MIX1]
            act.wait_ge(o_gmm, KC + 2)
            nc.scalar.activation(gas[:], bank[2][0:16, :], ACT.Copy).then_inc(o_ga, 1)
            act_take(act, "odd_in", 0, 8, oin)
            act_take(act, "odd_in", 8, 8, oin, lambda i, j: i * 2 + (8 + j), ACT.Silu)
            act_take(act, "odd_in", 16, 8, oin, lambda i, j: i * 2 + (16 + j))
            act.preload_act_table_set(LOG_EXP)
            for hd in range(4):
                act.wait_ge(o_al, hd + 1)
                if hd:
                    act.wait_ge(o_mn, 2 * hd)
                nc.scalar.activation(oa[:], bank[3 + hd][:], ACT.Abs, bias=obias[:, hd:hd + 1]).then_inc(o_ab, 1)
                act.wait_ge(o_ab, 2 * hd + 1)
                nc.scalar.activation(oa[:], oa[:], ACT.Exp, scale=-1.0).then_inc(o_ab, 1)
                act.wait_ge(o_ab, 2 * hd + 2)
                nc.scalar.activation(oa[:], oa[:], ACT.Ln, bias=ones[:, 0:1]).then_inc(o_l, 1)
            with act.Fori(0, 4) as i:
                act.wait_ge(o_lo, nth(i, 2, -1, 1))
                act.wait_ge(o_cum, 4)
                c_i = tile_of(cum, i)
                nc.scalar.activation(oe[:, 0, :], c_i, ACT.Exp, scale=1.0 / 16).then_inc(o_e, 1)
                nc.scalar.activation(oe[:, 1, :], c_i, ACT.Exp, scale=-1.0 / 16).then_inc(o_e, 1)
                act.wait_ge(o_df, nth(i, 1, 0))
                nc.scalar.activation(oe[:, 2, :], oe[:, 2, :], ACT.Exp, scale=1.0 / 16).then_inc(o_e, 1)
                act.wait_ge(o_tr, nth(i, 1, 0))
                nc.scalar.activation(kdt[:], bank[5][:], ACT.Copy).then_inc(o_kt, 1)
                act.wait_ge(o_o, nth(i, 1, 0, 1))
                for e in range(2):
                    nc.scalar.activation(osq[:, e, :], acc[e][:], ACT.Square).then_inc(o_sq, 1)
                act.wait_ge(o_ms, nth(i, 1, 0))
                nc.scalar.activation(orr[:], bank[4][:], ACT.Ln, bias=epsc, scale=1.0 / 256).then_inc(o_ln, 1)
                act.wait_ge(o_ln, nth(i, 1, 0))
                nc.scalar.activation(orr[:], orr[:], ACT.Exp, scale=-0.5).then_inc(o_r, 1)
                for e in range(2):
                    act.wait_ge(o_mix, nth(i, 2, e))
                    nc.scalar.activation(tile_of(xh, i * 2 + e), omix[:, e, :], ACT.Copy).then_inc(o_hi, 1)

        def dve_odd(dve):
            splits_only(dve, "odd_in", 0, 24)
            nc.vector.memset(att[:], 0.0).then_inc(o_am, 1)
            for hd in range(4):
                dve.wait_ge(o_al, hd + 1)
                dve.wait_ge(o_ab, 2 * hd + 1)
                nc.vector.tensor_scalar(omin[:], bank[3 + hd][:], obias[:, hd:hd + 1], 0.0, ALU.add,
                                        ALU.min).then_inc(o_mn, 1)
                dve.wait_ge(o_mn, 2 * hd + 1)
                dve.wait_ge(o_l, hd + 1)
                nc.vector.tensor_tensor(omin[:], omin[:], oa[:], ALU.subtract).then_inc(o_mn, 1)
                dve.wait_ge(o_mn, 2 * hd + 2)
                nc.vector.tensor_tensor_scan(cum[:, hd, :], restart, omin[:], 0.0, ALU.mult, ALU.add).then_inc(o_cum, 1)
                dve.wait_ge(o_cum, hd + 1)
            dve.wait_ge(acc_free[0], freed(O0["odd_in"] + 22))
            dve.wait_ge(acc_free[1], freed(O0["odd_in"] + 23))
            with dve.Fori(0, 4) as i:
                dve.wait_ge(o_o, nth(i, 1, -1, 1))
                dve.wait_ge(o_lo, nth(i, 2, -1, 1))
                c_i = cum[:, ds(i, 1), :].rearrange("p a (c t) -> p (a c) t", t=CH)
                nc.vector.tensor_tensor(oe[:, 2, :].rearrange("p (c t) -> p c t", t=CH),
                                        c_i[:, :, CH - 1:CH].broadcast_to([P, NCH, CH]), c_i,
                                        ALU.subtract).then_inc(o_df, 1)
                for e in range(2):
                    nc.vector.tensor_copy(vo[:, e, :], tile_of(oin, i * 2 + (16 + e))).then_inc(o_v, 1)
                dve.wait_ge(o_e, nth(i, 3, 0))
                nc.vector.scalar_tensor_tensor(qt[:], tile_of(oin, i), float(P) ** -0.5, oe[:, 0, :],
                                               ALU.mult, ALU.mult).then_inc(o_qk, 1)
                dve.wait_ge(o_e, nth(i, 3, 1))
                nc.vector.tensor_tensor(kt[:], tile_of(oin, i + 4), oe[:, 1, :], ALU.mult).then_inc(o_qk, 1)
                dve.wait_ge(o_at, nth(i, 1, 0))
                dve.wait_ge(o_e, nth(i, 3, 2))
                nc.vector.tensor_tensor(kd[:], tile_of(oin, i + 4), oe[:, 2, :], ALU.mult).then_inc(o_qk, 1)
                nc.vector.copy_predicated(att[:], causal.bitcast(mybir.dt.uint32), bank[6][:]).then_inc(o_am, 1)
                dve.wait_ge(o_c, nth(i, 7, 6))
                for c in range(NCH - 1):
                    got = of_chunk(c)
                    if c == 0:
                        nc.vector.tensor_copy(state[:, 0, :], got).then_inc(o_s, 1)
                    else:
                        dve.wait_ge(o_s, nth(i, 7, c - 1))
                        nc.vector.scalar_tensor_tensor(state[:, c, :], state[:, c - 1, :],
                                                       oe[:, 0, (c + 1) * CH - 1:(c + 1) * CH], got,
                                                       ALU.mult, ALU.add).then_inc(o_s, 1)
                dve.wait_ge(o_r, nth(i, 1, 0))
                for e in range(2):
                    nc.vector.scalar_tensor_tensor(omix[:, e, :], acc[e][:], obias[:, 4 + e:5 + e], orr[:],
                                                   ALU.mult, ALU.mult).then_inc(o_m, 1)
                for e in range(2):
                    dve.wait_ge(o_m, nth(i, 2, e))
                    nc.vector.tensor_tensor(omix[:, e, :], omix[:, e, :], tile_of(oin, i * 2 + (8 + e)),
                                            ALU.mult).then_inc(o_mix, 1)
                for e in range(2):
                    dve.wait_ge(o_hi, nth(i, 2, e))
                    nc.vector.tensor_tensor(tile_of(xl, i * 2 + e), omix[:, e, :], tile_of(xh, i * 2 + e).bitcast(F32),
                                            ALU.subtract).then_inc(o_lo, 1)

        used[0] = base
        GP = 32
        NA, NB = S // 32, 32
        su = at("su", [P, KC + 1, S])
        sz = at("sz", [P, KC, S])
        par = at("par", [P, 3, GP])
        sd = at("sd", [P, KC + 1])
        loop_base = used[0]
        sbc = at("sbc", [P, 4, GP + 4, 16])
        spt = at("spt", [P, 20, GP])
        pw = at("pw", [P, 2, 9, GP])
        tb = at("tb", [P, 2, GP, NB])
        ta = at("ta", [P, 2, GP, NA])
        se = at("se", [P, 2, 2, S])
        setmp = at("setmp", [P, 2, S])
        sp_ = at("sp_", [P, 4, S])
        sx = at("sx", [P, 2, 2, S])
        xb = at("xb", [P, 2, 640])
        xc = at("xc", [P, 2, 2, 640])
        xd = at("xd", [P, 2, P])
        bt = at("bt", [P, 2, S])
        used[0] = loop_base
        gh = at("gh", [P, KC, S], F32R)
        gl = at("gl", [P, KC, S], F32R)
        sgf = at("sgf", [P, 2, S])
        sg = at("sg", [P, S])
        g1 = at("g1", [P, S])
        g2 = at("g2", [P, S])
        s_loaded = sem("s_loaded")
        s_par = sem("s_par")
        s_pow2 = sem("s_pow2")
        s_x = sem("s_x")
        s_tr = sem("s_tr")
        s_bt = sem("s_bt")
        s_bu = sem("s_bu")
        s_e = sem("s_e")
        s_e0 = sem("s_e0")
        s_p = sem("s_p")
        s_free = sem("s_free")
        s_r = sem("s_r")
        s_v = sem("s_v")
        s_q = sem("s_q")
        s_xre = sem("s_xre")
        s_xim = sem("s_xim")
        s_y = sem("s_y")
        s_yo = sem("s_yo")
        s_gel = sem("s_gel")
        s_gh = sem("s_gh")
        s_gl = sem("s_gl")
        s_g1 = sem("s_g1")
        s_g2 = sem("s_g2")
        s_oh = sem("s_oh")
        s_ol = sem("s_ol")
        setup_steps = [0]
        FACT = [1.0, 1.0, 2.0, 6.0, 24.0, 120.0, 720.0, 5040.0, 40320.0, 362880.0]
        MAGIC = 1.5 * 2.0 ** 23

        def s5_loads(act):
            for to, what in ((par[:], "s5_par"), (sbc[:], "s5_bc"), (sd[:], "s5_d")):
                act.dma_start(to, A[what]).then_inc(s_loaded, 16)

        def after_last(dve):
            if setup_steps[0]:
                dve.wait_ge(s_par, setup_steps[0])
            setup_steps[0] += 1

        def tt(dve, to, a, b, op):
            after_last(dve)
            nc.vector.tensor_tensor(to, a, b, op).then_inc(s_par, 1)

        def ts(dve, to, a, s1, s2, op1, op2):
            after_last(dve)
            nc.vector.tensor_scalar(to, a, s1, s2, op1, op2).then_inc(s_par, 1)

        def stt(dve, to, a, s1, b, op1, op2):
            after_last(dve)
            nc.vector.scalar_tensor_tensor(to, a, s1, b, op1, op2).then_inc(s_par, 1)

        lg_dt, lam_re, lam_im = (par[:, j, :] for j in range(3))
        (kk, rr, qq, p2, dt_, xx, ee, th, yy, zz, ss, vv, mag, abim, nr, den, cre, cim, t1, t2) = \
            (spt[:, j, :] for j in range(20))
        POW2_STEP = 2

        def polynomial(dve, to, x, coefs):
            ts(dve, to, x, coefs[0], 0.0, ALU.mult, ALU.add)
            for c in coefs[1:]:
                stt(dve, to, to, c, x, ALU.add, ALU.mult)

        def s5_rates(dve):
            dve.wait_ge(s_loaded, 48)
            ts(dve, kk, lg_dt, 1.4426950408889634, MAGIC, ALU.mult, ALU.add)
            ts(dve, kk, kk, -MAGIC, 0.0, ALU.add, ALU.add)
            stt(dve, rr, kk, -0.693359375, lg_dt, ALU.mult, ALU.add)
            stt(dve, rr, kk, 2.12194440e-4, rr, ALU.mult, ALU.add)
            polynomial(dve, qq, rr, [1.0 / FACT[k] for k in range(7, 0, -1)])
            dve.wait_ge(s_pow2, 1)
            ts(dve, t1, p2, 2.0 ** 20 + 1, 0.0, ALU.mult, ALU.add)
            tt(dve, t2, t1, p2, ALU.subtract)
            tt(dve, p2, t1, t2, ALU.subtract)
            stt(dve, dt_, qq, 1.0, p2, ALU.add, ALU.mult)
            ts(dve, lam_re, lam_re, -1e-4, 0.0, ALU.min, ALU.add)
            tt(dve, xx, lam_re, dt_, ALU.mult)
            ts(dve, xx, xx, -80.0, 1.0 / 64, ALU.max, ALU.mult)
            polynomial(dve, ee, xx, [1.0 / FACT[k] for k in range(7, 0, -1)])
            for _ in range(6):
                stt(dve, ee, ee, 2.0, ee, ALU.add, ALU.mult)
            ts(dve, mag, ee, 1.0, 0.0, ALU.add, ALU.add)

        def s5_angles(dve):
            tt(dve, th, lam_im, dt_, ALU.mult)
            ts(dve, kk, th, 0.15915494309189535, MAGIC, ALU.mult, ALU.add)
            ts(dve, kk, kk, -MAGIC, 0.0, ALU.add, ALU.add)
            stt(dve, rr, kk, -6.28125, th, ALU.mult, ALU.add)
            stt(dve, rr, kk, -0.0019350051879882812, rr, ALU.mult, ALU.add)
            stt(dve, rr, kk, -3.0199157663446332e-07, rr, ALU.mult, ALU.add)
            ts(dve, yy, rr, 0.125, 0.0, ALU.mult, ALU.add)
            tt(dve, zz, yy, yy, ALU.mult)
            polynomial(dve, ss, zz, [1 / FACT[9], -1 / FACT[7], 1 / FACT[5], -1 / FACT[3]])
            stt(dve, ss, ss, 1.0, yy, ALU.add, ALU.mult)
            polynomial(dve, vv, zz, [-1 / FACT[8], 1 / FACT[6], -1 / FACT[4], 1 / FACT[2]])
            for _ in range(3):
                stt(dve, t1, vv, -1.0, ss, ALU.add, ALU.mult)
                stt(dve, vv, ss, 2.0, ss, ALU.mult, ALU.mult)
                ts(dve, ss, t1, -2.0, 0.0, ALU.mult, ALU.add)

        def s5_inputs(dve):
            tt(dve, abim, mag, ss, ALU.mult)
            tt(dve, t1, vv, mag, ALU.mult)
            tt(dve, nr, ee, t1, ALU.subtract)
            tt(dve, t1, lam_re, lam_re, ALU.mult)
            tt(dve, t2, lam_im, lam_im, ALU.mult)
            tt(dve, den, t1, t2, ALU.add)
            after_last(dve)
            nc.vector.reciprocal(den, den).then_inc(s_par, 1)
            for to, a, b, op in ((cre, nr, abim, ALU.add), (cim, abim, nr, ALU.subtract)):
                tt(dve, t1, a, lam_re, ALU.mult)
                tt(dve, t2, b, lam_im, ALU.mult)
                tt(dve, t1, t1, t2, op)
                tt(dve, to, t1, den, ALU.mult)
            c_r, c_i = (c.rearrange("p (g a) -> p g a", a=1).broadcast_to([P, GP, 16]) for c in (cre, cim))
            b_r, b_i = sbc[:, 0, 0:GP, :], sbc[:, 1, 0:GP, :]
            w = [sp_[:, j, :].rearrange("p (g c) -> p g c", c=16) for j in range(4)]
            tt(dve, w[0], c_r, b_r, ALU.mult)
            tt(dve, w[1], c_i, b_i, ALU.mult)
            tt(dve, w[2], c_r, b_i, ALU.mult)
            tt(dve, w[3], c_i, b_r, ALU.mult)
            tt(dve, b_r, w[0], w[1], ALU.subtract)
            tt(dve, b_i, w[2], w[3], ALU.add)

        def s5_powers(dve):
            ts(dve, pw[:, 0, 0, :], vv, -1.0, 1.0, ALU.mult, ALU.add)
            ts(dve, pw[:, 1, 0, :], ss, 1.0, 0.0, ALU.mult, ALU.add)
            for m in range(1, 9):
                re, im = pw[:, 0, m - 1, :], pw[:, 1, m - 1, :]
                tt(dve, t1, re, re, ALU.mult)
                tt(dve, t2, im, im, ALU.mult)
                tt(dve, kk, t1, t2, ALU.add)
                ts(dve, kk, kk, -1.0, 2.0, ALU.mult, ALU.add)
                tt(dve, rr, t1, t2, ALU.subtract)
                tt(dve, pw[:, 0, m, :], rr, kk, ALU.mult)
                stt(dve, qq, re, 2.0, im, ALU.mult, ALU.mult)
                tt(dve, pw[:, 1, m, :], qq, kk, ALU.mult)

        def s5_table(dve, to, count, m0):
            after_last(dve)
            nc.vector.memset(to[:, 0, :, 0:1], 1.0).then_inc(s_par, 1)
            after_last(dve)
            nc.vector.memset(to[:, 1, :, 0:1], 0.0).then_inc(s_par, 1)
            n, m = 1, m0
            while n < count:
                w_r, w_i = (pw[:, c, m, :].rearrange("p (g a) -> p g a", a=1).broadcast_to([P, GP, n]) for c in range(2))
                t_r, t_i = to[:, 0, :, 0:n], to[:, 1, :, 0:n]
                w = [sp_[:, j, 0:GP * n].rearrange("p (g c) -> p g c", c=n) for j in range(4)]
                tt(dve, w[0], t_r, w_r, ALU.mult)
                tt(dve, w[1], t_i, w_i, ALU.mult)
                tt(dve, w[2], t_r, w_i, ALU.mult)
                tt(dve, w[3], t_i, w_r, ALU.mult)
                tt(dve, to[:, 0, :, n:2 * n], w[0], w[1], ALU.subtract)
                tt(dve, to[:, 1, :, n:2 * n], w[2], w[3], ALU.add)
                n, m = 2 * n, m + 1

        def s5_spread(dve, i, f):
            for half in range(2):
                rows = slice(64 * half, 64 * half + 64)

                def spread(x):
                    return x[rows, :].rearrange("p (q w) -> p q w", w=160)[:, :, 16 * half:16 * half + 16]

                pairs = ds(i * 16 + 4 * f, 4)
                for c in range(2):
                    nc.vector.tensor_copy(spread(xb[:, c, :]), sbc[rows, c, pairs, :]).then_inc(s_x, 1)
                nc.vector.tensor_copy(spread(xc[:, f % 2, 0, :]), sbc[rows, 2, pairs, :]).then_inc(s_x, 1)
                nc.vector.tensor_scalar(spread(xc[:, f % 2, 1, :]), sbc[rows, 3, pairs, :], -1.0, 0.0,
                                        ALU.mult, ALU.add).then_inc(s_x, 1)
            nc.vector.tensor_scalar(xd[:, f % 2, :], ident, sd[:, ds(i * 4 + f, 1)], 0.0, ALU.mult,
                                    ALU.add).then_inc(s_x, 1)

        def dve_s5(dve):
            t0 = T0["s5_in"]
            for j in range(KC):
                dve.wait_ge(tile_done, t0 + j + 1)
                split_tile(dve, (j + 2) % 4, (t0 + j + 2) // 4)
                if j == 0:
                    s5_rates(dve)
                if j == 1:
                    s5_angles(dve)
                if j == 2:
                    s5_inputs(dve)
                if j == 3:
                    s5_powers(dve)
                if j == 4:
                    s5_table(dve, tb, NB, 0)
                if j == 5:
                    s5_table(dve, ta, NA, 5)
                if j == 6:
                    for x in (xb[:], xc[:], su[:, KC, :]):
                        after_last(dve)
                        nc.vector.memset(x, 0.0).then_inc(s_par, 1)
                    dve.wait_ge(s_par, setup_steps[0])
                    s5_spread(dve, 0, 0)
            with dve.Fori(0, 2) as i:
                for f in range(4):
                    for q in range(4):
                        g = 4 * f + q
                        a, b, c, d = (sp_[:, j, :] for j in range(4))
                        e_r, e_i = se[:, q % 2, 0, :], se[:, q % 2, 1, :]
                        b_r, b_i = bank[2 + q % 2], bank[4 + q % 2]
                        dve.wait_ge(s_bu, nth(i, 16, g))
                        dve.wait_ge(s_e, nth(i, 96, 6 * g + 5, 1))
                        dve.wait_ge(s_xim, nth(i, 16, g - 1, 2))
                        nc.vector.tensor_tensor(a, b_r[:], e_r, ALU.mult).then_inc(s_p, 1)
                        nc.vector.tensor_tensor(b, b_i[:], e_i, ALU.mult).then_inc(s_p, 1)
                        nc.vector.tensor_tensor(c, b_i[:], e_r, ALU.mult).then_inc(s_p, 1)
                        nc.vector.tensor_tensor(d, b_r[:], e_i, ALU.mult).then_inc(s_free, 1)
                        dve.wait_ge(s_p, nth(i, 48, 3 * g + 1))
                        nc.vector.tensor_tensor(a, a, b, ALU.add).then_inc(s_r, 1)
                        dve.wait_ge(s_free, nth(i, 16, g, 1))
                        nc.vector.tensor_tensor(c, c, d, ALU.subtract).then_inc(s_r, 1)
                        decay_g = mag[:, ds(i * 16 + g, 1)].broadcast_to([P, S])
                        dve.wait_ge(s_r, nth(i, 32, 2 * g))
                        nc.vector.tensor_tensor_scan(b, decay_g, a, 0.0, ALU.mult, ALU.add).then_inc(s_v, 1)
                        dve.wait_ge(s_r, nth(i, 32, 2 * g + 1))
                        nc.vector.tensor_tensor_scan(d, decay_g, c, 0.0, ALU.mult, ALU.add).then_inc(s_v, 1)
                        dve.wait_ge(s_v, nth(i, 32, 2 * g))
                        nc.vector.tensor_tensor(a, b, e_r, ALU.mult).then_inc(s_q, 1)
                        dve.wait_ge(s_v, nth(i, 32, 2 * g + 1))
                        nc.vector.tensor_tensor(c, d, e_i, ALU.mult).then_inc(s_q, 1)
                        dve.wait_ge(s_q, nth(i, 64, 4 * g + 1))
                        dve.wait_ge(s_y, nth(i, 16, g - 2, 2))
                        nc.vector.tensor_tensor(sx[:, q % 2, 0, :], a, c, ALU.subtract).then_inc(s_xre, 1)
                        dve.wait_ge(s_xre, nth(i, 16, g))
                        nc.vector.tensor_tensor(a, b, e_i, ALU.mult).then_inc(s_q, 1)
                        nc.vector.tensor_tensor(c, d, e_r, ALU.mult).then_inc(s_q, 1)
                        dve.wait_ge(s_q, nth(i, 64, 4 * g + 3))
                        nc.vector.tensor_tensor(sx[:, q % 2, 1, :], a, c, ALU.add).then_inc(s_xim, 1)
                        if q == 1:
                            dve.wait_ge(s_tr, nth(i, 8, 2 * f + 1))
                            dve.wait_ge(s_y, nth(i, 16, 4 * f - 1, 2))
                            s5_spread(dve, i, f + 1)
                        if q == 2:
                            dve.wait_ge(tile_done, i * 4 + (t0 + 8 + f + 1))
                            split_tile(dve, (f + 2) % 4, i + ((t0 + 8 + f + 2) // 4))
            with dve.Fori(0, 4) as i:
                for j in range(2):
                    dve.wait_ge(s_gh, nth(i, 2, j))
                    nc.vector.tensor_tensor(tile_of(xl, i * 2 + j), sgf[:, j, :], tile_of(xh, i * 2 + j).bitcast(F32),
                                            ALU.subtract).then_inc(s_gl, 1)
            t0 = T0["s5_glu"]
            with dve.Fori(0, 4) as i:
                for j in range(2):
                    dve.wait_ge(tile_done, i * 4 + (t0 + 2 * j + 1))
                    split_tile(dve, (2 * j + 2) % 4, i + ((t0 + 2 * j + 2) // 4))
                    dve.wait_ge(tile_done, i * 4 + (t0 + 2 * j + 2))
                    split_tile(dve, (2 * j + 3) % 4, i + ((t0 + 2 * j + 3) // 4))
                    dve.wait_ge(acc_free[1], freed(O0["s5_glu"] + 2 * j + 1, i, 2))
                    nc.vector.tensor_tensor(g1[:], sg[:], acc[0][:], ALU.mult).then_inc(acc_free[0], 1)
                    dve.wait_ge(acc_free[0], freed(O0["s5_glu"] + 2 * j, i, 2))
                    nc.vector.tensor_tensor(g2[:], g1[:], tile_of(sz, i * 2 + j), ALU.mult).then_inc(s_g2, 1)
                    dve.wait_ge(s_oh, nth(i, 2, j))
                    nc.vector.tensor_tensor(tile_of(gl, i * 2 + j), g2[:], tile_of(gh, i * 2 + j).bitcast(F32),
                                            ALU.subtract).then_inc(s_ol, 1)
            dve_residual(dve, "s5_out")

        def pool_s5(pool):
            t0 = T0["s5_in"] + 8
            with pool.Fori(0, 2) as i:
                for f in range(4):
                    pool.wait_ge(w_hi, i * 4 + (t0 + f + 1))
                    nc.gpsimd.tensor_tensor(wlo[:, f % 2, :], raw[:, f, :], whi[:, f % 2, :].bitcast(F32),
                                            ALU.subtract).then_inc(w_lo, 1)
                    for q in range(4):
                        g = 4 * f + q
                        a_r, a_i = (ta[:, c, ds(i * 16 + g, 1), :].rearrange("p o a -> p a o")
                                    .broadcast_to([P, NA, NB]) for c in range(2))
                        b_r, b_i = (tb[:, c, ds(i * 16 + g, 1), :].broadcast_to([P, NA, NB]) for c in range(2))
                        e_r, e_i = (se[:, q % 2, c, :].rearrange("p (a b) -> p a b", b=NB) for c in range(2))
                        t, u = (setmp[:, c, :].rearrange("p (a b) -> p a b", b=NB) for c in range(2))
                        if f == 0 and q == 0:
                            pool.wait_ge(s_x, 1)
                        pool.wait_ge(s_e, nth(i, 96, 6 * g - 1, 1))
                        pool.wait_ge(s_xim, nth(i, 16, g - 2, 2))
                        nc.gpsimd.tensor_tensor(seedt[:, 40:41], epsc, epsc, ALU.add).then_inc(s_e0, 1)
                        nc.gpsimd.tensor_tensor(e_r, a_r, b_r, ALU.mult).then_inc(s_e, 1)
                        nc.gpsimd.tensor_tensor(t, a_i, b_i, ALU.mult).then_inc(s_e, 1)
                        nc.gpsimd.tensor_tensor(e_i, a_r, b_i, ALU.mult).then_inc(s_e, 1)
                        nc.gpsimd.tensor_tensor(u, a_i, b_r, ALU.mult).then_inc(s_e, 1)
                        pool.wait_ge(s_e, nth(i, 96, 6 * g + 1, 1))
                        nc.gpsimd.tensor_tensor(e_r, e_r, t, ALU.subtract).then_inc(s_e, 1)
                        pool.wait_ge(s_e, nth(i, 96, 6 * g + 3, 1))
                        nc.gpsimd.tensor_tensor(e_i, e_i, u, ALU.add).then_inc(s_e, 1)

        def pe_s5(pe):
            t0, o0 = T0["s5_in"], O0["s5_in"]
            pe_normed(pe, ORDER[N_S5])
            products_feature_major(pe, "s5_in", 0, 8)

            def transposes(c):
                for q in range(4):
                    mm = nc.tensor.transpose(bank[7][:, q * P:(q + 1) * P], xb[:, c, q * P:(q + 1) * P], ident)
                mm.then_inc(s_tr, 1)

            def inputs(i, f, q):
                for c in range(2):
                    mm = nc.tensor.matmul(bank[2 + 2 * c + q % 2][:], bt[:, c, q * P:(q + 1) * P],
                                          tile_of(su, i * 4 + f), start=True, stop=True)
                mm.then_inc(s_bu, 1)

            pe.wait_ge(s_x, 9)
            pe.wait_ge(acc_free[0], freed(o0 + 6))
            pe.wait_ge(acc_free[1], freed(o0 + 7))
            transposes(0)
            pe.wait_ge(s_bt, 1)
            transposes(1)
            pe.wait_ge(s_bt, 2)
            for c in range(2):
                mm = nc.tensor.matmul(bank[2 + 2 * c][:], bt[:, c, 0:P], su[:, 0, :], start=True, stop=True)
            mm.then_inc(s_bu, 1)
            with pe.Fori(0, 2) as i:
                for f in range(4):
                    def outputs(q):
                        pe.wait_ge(s_xim, nth(i, 16, 4 * f + q, 2))
                        if q == 0:
                            pe.wait_ge(s_yo, nth(i, 4, f - 1, 1))
                            nc.tensor.matmul(bank[6][:], xd[:, f % 2, :], tile_of(su, i * 4 + f), start=True, stop=False)
                        for c in range(2):
                            mm = nc.tensor.matmul(bank[6][:], xc[:, f % 2, c, q * P:(q + 1) * P], sx[:, q % 2, c, :],
                                                  start=False, stop=c == 1 and q == 3)
                        mm.then_inc(s_y, 1)

                    pe.wait_ge(s_free, nth(i, 16, 4 * f - 1, 1))
                    inputs(i, f, 1)
                    pe.wait_ge(w_lo, i * 4 + (t0 + 8 + f + 1))
                    pe.wait_ge(acc_free[f % 2], i * 2 + ((o0 + 8 + f) // 2 + 1))
                    product(pe, f % 2, acc[f % 2][:], lambda k: xh[:, k, :], lambda k: xl[:, k, :],
                            KC, True, True).then_inc(tile_done, 1)
                    outputs(0)
                    pe.wait_ge(s_free, nth(i, 16, 4 * f, 1))
                    inputs(i, f, 2)
                    outputs(1)
                    pe.wait_ge(s_free, nth(i, 16, 4 * f + 1, 1))
                    inputs(i, f, 3)
                    pe.wait_ge(s_x, nth(i, 36, 9 * f + 17))
                    transposes(0)
                    pe.wait_ge(s_bt, nth(i, 8, 2 * f + 2))
                    transposes(1)
                    outputs(2)
                    pe.wait_ge(s_bt, nth(i, 8, 2 * f + 3))
                    pe.wait_ge(s_free, nth(i, 16, 4 * f + 2, 1))
                    inputs(i, f + 1, 0)
                    outputs(3)
            pe.wait_ge(s_gl, KC + 2)
            products_feature_major(pe, "s5_glu", 0, 16)
            pe.wait_ge(s_ol, KC)
            pe_residual(pe, "s5_out", ORDER[N_FINAL], rhs=[(lambda k: gh[:, k, :], lambda k: gl[:, k, :])])

        def act_s5(act):
            t0, o0 = T0["s5_in"], O0["s5_in"]
            act.wait_ge(s_par, POW2_STEP)
            nc.scalar.activation(p2, kk, ACT.Exp, scale=float(np.log(2.0))).then_inc(s_pow2, 1)
            act_take(act, "s5_in", 0, 8, su)
            for c in range(2):
                act.wait_ge(s_tr, c + 1)
                nc.scalar.activation(bt[:, c, :], bank[7][:], ACT.Copy).then_inc(s_bt, 1)
            with act.Fori(0, 2) as i:
                for f in range(4):
                    act.wait_ge(tile_done, i * 4 + (t0 + 8 + f + 1))
                    nc.scalar.activation(tile_of(sz, i * 4 + f), acc[f % 2][:], ACT.Silu).then_inc(acc_free[f % 2], 1)
                    for c in range(2):
                        act.wait_ge(s_tr, nth(i, 8, 2 * f + 2 + c))
                        nc.scalar.activation(bt[:, c, :], bank[7][:], ACT.Copy).then_inc(s_bt, 1)
                    act.wait_ge(s_y, nth(i, 16, 4 * f + 3, 2))
                    nc.scalar.activation(tile_of(su, i * 4 + f), bank[6][:], ACT.Copy).then_inc(s_yo, 1)
            act.wait_ge(s_yo, KC + 1)
            with act.Fori(0, 4) as i:
                for j in range(2):
                    act.wait_ge(s_gl, nth(i, 2, j - 2, 2))
                    nc.scalar.activation(sgf[:, j, :], tile_of(su, i * 2 + j), ACT.Gelu_apprx_tanh).then_inc(s_gel, 1)
                    act.wait_ge(s_gel, nth(i, 2, j))
                    nc.scalar.activation(tile_of(xh, i * 2 + j), sgf[:, j, :], ACT.Copy).then_inc(s_gh, 1)
            with act.Fori(0, 4) as i:
                for j in range(2):
                    act.wait_ge(tile_done, i * 4 + (T0["s5_glu"] + 2 * j + 2))
                    act.wait_ge(acc_free[0], freed(O0["s5_glu"] + 2 * j - 2, i, 2))
                    nc.scalar.activation(sg[:], acc[1][:], ACT.Sigmoid).then_inc(acc_free[1], 1)
                    act.wait_ge(s_g2, nth(i, 2, j))
                    nc.scalar.activation(tile_of(gh, i * 2 + j), g2[:], ACT.Copy).then_inc(s_oh, 1)

        def dve_final_norm(dve, n):
            dve.wait_ge(rstd_ready, n + 1)
            with dve.Fori(0, KC // 2) as i:
                for j in range(2):
                    nc.vector.scalar_tensor_tensor(chunk(h, i * 2 + j), chunk(h, i * 2 + j),
                                                   gains[:, norms[n], ds(i * 2 + j, 1)], rstd[:],
                                                   ALU.mult, ALU.mult).then_inc(norm_f, 1)

        blocks = [(key, stage) for key, stage in ((N_NSA, "nsa"), (N_S5, "s5"), (N_FINAL, "final"), (N_MIX0, "even"), (N_FFN0, "ffn0"), (N_MIX1, "odd"), (N_FFN1, "ffn1"))
                  if key in norms]
        block = ctx.enter_context(nc.Block())

        @block.sync
        def _(sp):
            sp.dma_start(h[:], A["x"]).then_inc(x_landed, 16)
            sp_stream(sp)

        @block.gpsimd
        def _(pool):
            if "s5_in" in names:
                pool_stream(pool, 0, T0["s5_in"] + 8)
                pool_s5(pool)
                pool_stream(pool, T0["s5_glu"], TILES)
            else:
                pool_stream(pool, 0, TILES)

        @block.scalar
        def _(act):
            act.dma_start(tables[:], A["tables"]).then_inc(loaded, 16)
            act.dma_start(gains[:], A["gains"]).then_inc(loaded, 16)
            act.wait_ge(loaded, 32)
            act.wait_ge(zeroed, 1)
            act.wait_ge(x_landed, 16)
            act_all_squares(act, 0, x_landed, None)
            for key, name in blocks:
                n = ORDER[key]
                if name == "nsa":
                    nsa_loads(act)
                if name == "odd":
                    for to, what in ((otab, "odd_tables"), (wga, "wga"), (walpha, "walpha"), (obias, "odd_bias")):
                        act.dma_start(to[:], A[what]).then_inc(o_loaded, 16)
                if name == "s5":
                    s5_loads(act)
                act_rstd(act, n)
                if name == "final":
                    if n + 1 < len(norms):
                        act_all_squares(act, n + 1, norm_f, lambda m: m + (8 * n + 1))
                    continue
                act_norm_split(act, n)
                if name == "s5":
                    act_s5(act)
                    out_stage = "s5_out"
                if name == "nsa":
                    act_nsa(act)
                    out_stage = "nsa_out"
                if name == "even":
                    act_even(act)
                    out_stage = "even_out"
                if name == "odd":
                    act_odd(act)
                    out_stage = "odd_out"
                if name in ("ffn0", "ffn1"):
                    act_ffn(act, int(name[3]))
                    out_stage = "down" + name[3]
                if n + 1 < len(norms):
                    act_residual(act, out_stage, n + 1)
            for m in range(KC - 2, KC):
                act.wait_ge(acc_free[m % 2], freed(O0[out_stage] + m))
            if blocks[-1][1] == "final":
                act.wait_ge(norm_f, 8 * len(norms))
            act.dma_start(out, h[:]).then_inc(out_written, 16)
            act.wait_ge(out_written, 16)

        @block.tensor
        def _(pe):
            pe.wait_ge(loaded, 32)
            pe_all_squares(pe, 0)
            for key, name in blocks:
                n = ORDER[key]
                if name == "nsa":
                    pe_nsa(pe)
                    pe.wait_ge(n_lo, 9)
                    pe_residual(pe, "nsa_out", n + 1 if n + 1 < len(norms) else None)
                if name == "s5":
                    pe_s5(pe)
                if name == "final" and n + 1 < len(norms):
                    pe_all_squares(pe, n + 1)
                if name == "even":
                    pe_even(pe)
                    pe.wait_ge(r_lo, 4)
                    pe.wait_ge(e_ol, 5)
                    pe_residual(pe, "even_out", n + 1 if n + 1 < len(norms) else None)
                if name == "odd":
                    pe_odd(pe)
                    pe.wait_ge(o_lo, 9)
                    pe_residual(pe, "odd_out", n + 1 if n + 1 < len(norms) else None)
                if name in ("ffn0", "ffn1"):
                    pe_ffn(pe, int(name[3]))

        @block.vector
        def _(dve):
            nc.vector.memset(xzero[:], 0.0).then_inc(zeroed, 1)
            seeded = [acc_free[0], acc_free[1], conv2, norm_lo, norm_lo, e_o, e_ol, r_o, r_mix, o_lo, o_o,
                      o_gmm, o_gmm, n_gmm, n_gmm, n_lo,
                      s_free, s_e, s_yo, s_xim, s_xim, s_y, s_y, s_gl, s_gl]
            for n, one in enumerate(seeded):
                nc.vector.memset(seedt[:, n:n + 1], 0.0).then_inc(one, 1)
            split_tile(dve, 0, 0)
            split_tile(dve, 1, 0)
            dve.wait_ge(loaded, 32)
            for key, name in blocks:
                if name == "final":
                    dve_final_norm(dve, ORDER[key])
                    continue
                dve_norm(dve, ORDER[key], reader={"odd": o_gmm, "nsa": n_gmm}.get(name))
                if name == "nsa":
                    dve_nsa(dve)
                    dve_residual(dve, "nsa_out")
                if name == "s5":
                    dve_s5(dve)
                if name == "even":
                    dve_even(dve)
                    dve_residual(dve, "even_out")
                if name == "odd":
                    dve_odd(dve)
                    dve_residual(dve, "odd_out")
                if name in ("ffn0", "ffn1"):
                    dve_ffn(dve, int(name[3]))


def slabs(w):
    k, n = w.shape
    return w.reshape(8, P, n // P, P).transpose(2, 1, 0, 3).reshape(n // P, P, SLAB)
def down(w):
    f = w.shape[0]
    w = np.concatenate([w, np.zeros((3 * 1024 - f, w.shape[1]), w.dtype)])
    return np.stack([slabs(w[q * 1024:(q + 1) * 1024]) for q in range(3)], 1).reshape(-1, P, 1024)
def up(w):
    s = slabs(w); n = len(s) // 2
    return np.stack([s[:n], s[n:]], 1).reshape(-1, P, 1024)
def cols(v):
    return np.ascontiguousarray(v.reshape(-1, P).T)

def host_weights(I, names):
    out = []
    if 'nsa' in names:
        w = I['l0_w_in']
        heads = [g * 4 + r for j in range(2) for r in range(4) for g in (2 * j, 2 * j + 1)]
        byhead = lambda x: x.reshape(-1, 16, 64)[:, heads].reshape(-1, 1024)
        kc, vc, ks, vs, kw, vw = [w[:, 1024 + 256 * j:1280 + 256 * j] for j in range(6)]
        out += [slabs(x) for x in (kc, vc, ks, kw)]
        for m in (I['l0_cmp_k_w1'], I['l0_cmp_v_w1']):
            for half in range(2):
                out += [slabs(m[1024 * q:1024 * q + 1024, half * P:half * P + P]) for q in range(2)]
        out += [slabs(byhead(w[:, :1024])), slabs(byhead(w[:, 2608:3632])), slabs(vs), slabs(vw)]
        out += [slabs(I['l0_w_out'].reshape(16, 64, 1024)[heads].reshape(1024, 1024))]
    if 's5' in names:
        out += [slabs(I['l1_w_in']), up(I['l1_w_glu']), slabs(I['l1_w_out'])]
    if 'even' in names:
        w = I['even_w_in_2'][0]
        sbq, sbk, sbv, rq, rk, rv, rg = [w[:, j * 512:(j + 1) * 512] for j in range(7)]
        out += [slabs(x) for x in (sbq, sbk, rq, rk, rg, sbv, rv)] + [slabs(I['even_w_out_2'][0])]
    if 'ffn0' in names:
        out += [up(I['ffn_w_up_2'][0]), down(I['ffn_w_down_2'][0])]
    if 'odd' in names:
        w = I['odd_w_in_2'][0]
        out += [slabs(w[:, 0:2048][:, :1024]), slabs(w[:, 2048:3072]), slabs(w[:, 1024:2048]), slabs(I['odd_w_out_2'][0])]
    if 'ffn1' in names:
        out += [up(I['ffn_w_up_2'][1]), down(I['ffn_w_down_2'][1])]
    return np.concatenate(out)

def host_tables():
    t = np.zeros((P, 2 * P + 8), np.float32)
    t[:, :P] = 1
    t[:, P:2 * P] = np.eye(P)
    t[:, 2 * P] = 1e-6
    return t

def host_even_tables():
    p, c = np.arange(P)[:, None], np.arange(P)[None, :]
    bd = (p // 64 == c // 64) / 64.0
    later = p > c
    before = p < c
    half = 64
    inv = np.float32(10000.0) ** (-np.arange(half, dtype=np.float32) / np.float32(half))
    ang = (np.arange(S, dtype=np.float32)[:, None] * inv[None, :]).astype(np.float32)
    cos, sin = np.cos(ang).T, np.sin(ang).T
    cc, sc = np.concatenate([cos, cos]), np.concatenate([sin, sin])
    dec = []
    for r in range(4):
        lg = np.log(1.0 - 2.0 ** (-5.0 - r))
        d = np.arange(S)[None, :] - p
        dec.append(np.where(d >= 0, np.exp(lg * np.maximum(d, 0)) * P ** -0.5, 0.0))
    return np.concatenate([bd, later, before, cc, sc, *dec, np.full((P, 4), 64e-6)], 1).astype(np.float32)

def host_swap():
    w = np.zeros((P, P), np.float32)
    for m in range(64):
        w[m + 64, m] = -1
        w[m, m + 64] = 1
    return w

def by_state(v):
    n = v.ndim
    return v.reshape((32, 2, 64) + v.shape[2:]).transpose((1, 2, 0) + tuple(range(3, n + 1))).reshape((P, 32) + v.shape[2:])
def s5_par(log_dt, lre, lim):
    dt = np.broadcast_to(log_dt[:, None], (64, 64))
    return np.ascontiguousarray(np.stack([by_state(v) for v in (dt, lre, lim)], 1))
def s5_bc(br, bi, cr, ci):
    t = np.zeros((P, 4, 36, 16), np.float32)
    for j, v in enumerate((br, bi, cr.transpose(0, 2, 1), ci.transpose(0, 2, 1))):
        t[:, j, :32] = by_state(v)
    return t
def host_arrays(I, names):
    a = dict(weights=host_weights(I, names), tables=host_tables())
    g = np.zeros((P, 7, 8), np.float32)
    for n, v in enumerate([I['l0_norm'], I['l1_norm'], I['final_norm'], I['mix_norm_g_2'][0], I['ffn_norm_g_2'][0], I['mix_norm_g_2'][1], I['ffn_norm_g_2'][1]]):
        g[:, n] = cols(v)
    a['gains'] = g
    cv = np.zeros((P, 2, 4, 22), np.float32)
    for l in range(2):
        for j in range(3): cv[:, l, j] = cols(I['ffn_conv_w_2'][l, j])
        cv[:, l, 3] = cols(I['ffn_conv_b_2'][l])
    a['conv'] = cv
    a['even_tables'] = host_even_tables()
    a['swap'] = host_swap()
    q, k = I['sb_q_gain_2'][0], I['sb_k_gain_2'][0]
    a['even_gains'] = np.stack([np.concatenate([q, q]), np.concatenate([k, k]), I['ret_out_gain_2'][0]], 1)
    p, c = np.arange(P)[:, None], np.arange(S)[None, :] % P
    a['odd_tables'] = np.concatenate([np.broadcast_to(np.arange(S) % 64 != 0, (P, S)), (p <= c) & (p // 64 == c // 64)], 1).astype(np.float32)
    a['wga'] = np.ascontiguousarray(I['odd_w_in_2'][0][:, 3072:].reshape(8, P, 16).transpose(1, 0, 2))
    a['walpha'] = I['gla_w_alpha_2'][0]
    a['odd_bias'] = np.concatenate([cols(I['gla_b_alpha_2'][0]), cols(I['gla_out_gain_2'][0])], 1)
    heads = [g * 4 + r for j in range(2) for r in range(4) for g in (2 * j, 2 * j + 1)]
    p, c = np.arange(P)[:, None], np.arange(S)[None, :]
    dist = p + 384 - c
    n, t = np.arange(32)[None, None, :], (np.arange(4)[None, :] * P + p)[:, :, None]
    seen = (16 * n + 31 <= t) & (n < 31)
    cd = np.where(seen, -(t - (16 * n + 15.5)), -1e30).reshape(P, P)
    cm = seen.astype(np.float32).reshape(P, P)
    sl = np.exp2(-8.0 * (np.array(heads) + 1) / 16)
    a['nsa_tables'] = np.concatenate([np.where(dist >= 0, -dist, -1e30), cd, cm, cm, np.broadcast_to(sl, (P, 16))], 1).astype(np.float32)
    wg = I['l0_w_in'][:, 2560:2608].reshape(1024, 3, 16)[:, :, heads].transpose(0, 2, 1).reshape(8, P, 48)
    a['wgate'] = np.ascontiguousarray(wg.transpose(1, 0, 2))
    k2, v2 = I['l0_cmp_k_w2'], I['l0_cmp_v_w2']
    a['w2'] = np.ascontiguousarray(np.concatenate([k2, k2, v2], 1).reshape(2, P, 192).transpose(1, 0, 2))
    pe = np.stack([cols(I['l0_cmp_k_pe'].reshape(-1)), cols(I['l0_cmp_v_pe'].reshape(-1))], 1)
    a['pe'] = np.ascontiguousarray(np.stack([pe, pe], 3))
    a['s5_par'] = s5_par(I['l1_log_dt'], I['l1_lambda_re'], I['l1_lambda_im'])
    a['s5_bc'] = s5_bc(I['l1_b_re'], I['l1_b_im'], I['l1_c_re'], I['l1_c_im'])
    a['s5_d'] = np.concatenate([cols(I['l1_d'].reshape(-1)), np.zeros((P, 1), np.float32)], 1)
    a['x'] = np.ascontiguousarray(I['x'][0].T.reshape(8, P, S).transpose(1, 0, 2))
    return a


BLOCKS = ("nsa", "s5", "even", "ffn0", "odd", "ffn1")


def kernel(**inputs):
    import concourse.bacc as bacc
    from concourse.bass_utils import run_bass_kernel_spmd

    nc = bacc.Bacc("TRN2", target_bir_lowering=False, num_devices=1)
    laid_out = host_arrays({name: np.asarray(value) for name, value in inputs.items()}, BLOCKS)
    arrays, args = {}, {}
    for name, a in laid_out.items():
        arrays[f"in_{name}_dram"] = np.ascontiguousarray(a)
        args[name] = nc.dram_tensor(f"in_{name}_dram", a.shape, mybir.dt.from_np(a.dtype), kind="ExternalInput").ap()
    out = nc.dram_tensor("out_0_dram", (P, KC, S), F32, kind="ExternalOutput").ap()
    build(nc, args, out)
    r = run_bass_kernel_spmd(nc, [arrays], core_ids=[0])
    got = np.asarray(r.results[0]["out_0_dram"])
    return np.ascontiguousarray(got.transpose(1, 0, 2).reshape(D, S).T).reshape(1, S, D)
```
